# Optimizing a Trainium2 kernel written in Bass

```python
import math
import jax, jax.numpy as jnp
from jax import lax
import numpy as np

D_MODEL = 1024
BATCH = 1
SEQ = 1024
DEPTH = 2
DEC_BATCH = 8
DEC_SEQ = 4
PAST_LEN = 2048
PAGE_SIZE = 128

N_A_LAYERS = DEPTH // 2
N_B_LAYERS = DEPTH - N_A_LAYERS
HEAD_DIM = 64
HEADS_PER_GROUP = 4
DIL_GROUPS = ((128, 1), (512, 4), (2048, 16))
N_GROUPS = len(DIL_GROUPS)
N_HEADS = HEADS_PER_GROUP * N_GROUPS
ATT_WIDTH = N_HEADS * HEAD_DIM
PAD_MULT = math.lcm(*[w for w, _ in DIL_GROUPS])
N_BUCKETS = 32
MAX_DISTANCE = 2048
CONV_A_WIDTH = 31
D_FF = 2816
CONV_F_WIDTH = 3
N_MOD = 6
EPS = 1e-6
LN_EPS = 1e-5
NEG_INF = -1e30

kernel_name = 'yoco_conformer_dilated_attn_step'

def _rmsnorm(x, g):
    x32 = x.astype(jnp.float32)
    y = x32 * lax.rsqrt(jnp.mean(x32 * x32, axis=-1, keepdims=True) + EPS) * g.astype(jnp.float32)
    return y.astype(x.dtype)

def _dwconv(full, w):
    return lax.conv_general_dilated(full, w[:, None, :].astype(full.dtype), (1,), 'VALID',
                                    dimension_numbers=('NWC', 'WIO', 'NWC'),
                                    feature_group_count=full.shape[-1])

def _rel_bucket(dist):
    max_exact = N_BUCKETS // 2
    d = jnp.maximum(dist, 1).astype(jnp.float32)
    large = max_exact + (jnp.log(d / max_exact) / math.log(MAX_DISTANCE / max_exact)
                         * (N_BUCKETS - max_exact)).astype(jnp.int32)
    large = jnp.minimum(large, N_BUCKETS - 1)
    return jnp.where(dist < max_exact, dist, large)

def _group_bias(rel_bias, g, dil, span):
    dist = jnp.arange(span + 1, dtype=jnp.int32) * dil
    hs = slice(g * HEADS_PER_GROUP, (g + 1) * HEADS_PER_GROUP)
    return rel_bias[_rel_bucket(dist)][:, hs].astype(jnp.float32)

def _prompt_dilated(q, k, v, bias_g, dil, span):
    B, S, H, Dh = q.shape
    L = S // dil
    nb = L // span

    def to_blocks(t):
        return t.reshape(B, L, dil, H, Dh).transpose(0, 2, 1, 3, 4).reshape(B * dil, nb, span, H, Dh)

    def with_prev(t):
        prev = jnp.concatenate([jnp.zeros_like(t[:, :1]), t[:, :-1]], axis=1)
        return jnp.concatenate([prev, t], axis=2)

    qb = to_blocks(q)
    kk = with_prev(to_blocks(k))
    vv = with_prev(to_blocks(v))
    s = jnp.einsum('nbqhd,nbkhd->nbhqk', qb, kk).astype(jnp.float32) * (HEAD_DIM ** -0.5)
    qi = jnp.arange(span)[:, None]
    ki = jnp.arange(2 * span)[None, :]
    m = qi + span - ki
    valid = ((m >= 0) & (m <= span))[None] & ((jnp.arange(nb)[:, None, None] > 0) | (ki >= span)[None])
    bias = jnp.transpose(bias_g[jnp.clip(m, 0, span)], (2, 0, 1))
    logits = jnp.where(valid[None, :, None], s + bias[None, None], NEG_INF)
    lse = jax.nn.logsumexp(logits, axis=-1)
    p = jnp.exp(logits - lse[..., None])
    o = jnp.einsum('nbhqk,nbkhd->nbqhd', p.astype(v.dtype), vv)
    o = o.reshape(B, dil, L, H, Dh).transpose(0, 2, 1, 3, 4).reshape(B, S, H, Dh)
    lse = lse.transpose(0, 1, 3, 2).reshape(B, dil, L, H).transpose(0, 2, 1, 3).reshape(B, S, H)
    return o, lse

def _sample_dilated(q, k_all, v_all, bias_g, dil, span):
    N, T, H, Dh = q.shape
    W = k_all.shape[1] - T
    idx = W + jnp.arange(T)[:, None] - jnp.arange(span + 1)[None, :] * dil
    valid = idx >= 0
    idx = jnp.maximum(idx, 0)
    kg = k_all[:, idx]
    vg = v_all[:, idx]
    s = jnp.einsum('nthd,ntmhd->nhtm', q, kg).astype(jnp.float32) * (HEAD_DIM ** -0.5)
    logits = jnp.where(valid[None, None], s + bias_g.T[None, :, None, :], NEG_INF)
    lse = jax.nn.logsumexp(logits, axis=-1)
    p = jnp.exp(logits - lse[..., None])
    o = jnp.einsum('nhtm,ntmhd->nthd', p.astype(v_all.dtype), vg)
    return o, lse.transpose(0, 2, 1)

def _conformer_conv(h, hist, w1, b1, dw, dwb, ln_g, ln_b, w2, b2):
    u = h @ w1 + b1
    a, g = jnp.split(u, 2, axis=-1)
    glu = a * jax.nn.sigmoid(g)
    full = jnp.concatenate([hist.astype(glu.dtype), glu], axis=1)
    y32 = (_dwconv(full, dw) + dwb).astype(jnp.float32)
    mu = jnp.mean(y32, axis=-1, keepdims=True)
    var = jnp.mean(jnp.square(y32 - mu), axis=-1, keepdims=True)
    y = (y32 - mu) * lax.rsqrt(var + LN_EPS) * ln_g.astype(jnp.float32) + ln_b.astype(jnp.float32)
    y = jax.nn.silu(y).astype(h.dtype)
    return y @ w2 + b2, full[:, -(CONV_A_WIDTH - 1):]

def _conv_ffn(h, hist, w_up, cw, cb, w_down):
    u = h @ w_up
    full = jnp.concatenate([hist.astype(u.dtype), u], axis=1)
    y = _dwconv(full, cw) + cb
    g, v = jnp.split(y, 2, axis=-1)
    return (jax.nn.silu(g) * v) @ w_down, full[:, -(CONV_F_WIDTH - 1):]

def _shared_kv(x, c_act, kv_bufs, buf_widths, prompt, p):
    N, T, _ = x.shape
    sh, sc = jnp.split((c_act @ p['w_mod_kv'] + p['b_mod_kv'])[:, None, :], 2, axis=-1)
    hkv = _rmsnorm(x, p['norm_kv']) * (1 + sc) + sh
    kv = (hkv @ p['w_kv']).reshape(N, T, 2, N_HEADS, HEAD_DIM)
    if prompt:
        s_pad = -(-T // PAD_MULT) * PAD_MULT
        kv_att = jnp.pad(kv, ((0, 0), (0, s_pad - T), (0, 0), (0, 0), (0, 0)))
    groups, bufs = [], []
    for g in range(N_GROUPS):
        hs = slice(g * HEADS_PER_GROUP, (g + 1) * HEADS_PER_GROUP)
        kv_g = kv[:, :, :, hs]
        W = buf_widths[g]
        if prompt:
            groups.append(kv_att[:, :, :, hs])
            if T >= W:
                bufs.append(kv_g[:, T - W:])
            else:
                bufs.append(jnp.pad(kv_g, ((0, 0), (W - T, 0), (0, 0), (0, 0), (0, 0))))
        else:
            full = jnp.concatenate([kv_bufs[g].astype(kv_g.dtype), kv_g], axis=1)
            groups.append(full)
            bufs.append(full[:, -W:])
    return groups, bufs

def _dilated_mixer(h, kv_groups, prompt, w_q, w_o, rel_bias):
    N, T, _ = h.shape
    q = (h @ w_q).reshape(N, T, N_HEADS, HEAD_DIM)
    if prompt:
        q = jnp.pad(q, ((0, 0), (0, kv_groups[0].shape[1] - T), (0, 0), (0, 0)))
    outs, lses = [], []
    for g, (window, dil) in enumerate(DIL_GROUPS):
        span = window // dil
        bias_g = _group_bias(rel_bias, g, dil, span)
        qg = q[:, :, g * HEADS_PER_GROUP:(g + 1) * HEADS_PER_GROUP]
        kg = kv_groups[g][:, :, 0]
        vg = kv_groups[g][:, :, 1]
        fn = _prompt_dilated if prompt else _sample_dilated
        o, lse = fn(qg, kg, vg, bias_g, dil, span)
        outs.append(o[:, :T])
        lses.append(lse[:, :T])
    o = jnp.stack(outs, axis=2)
    alpha = jax.nn.softmax(jnp.stack(lses, axis=2), axis=2)
    o = (o * alpha[..., None].astype(o.dtype)).reshape(N, T, ATT_WIDTH)
    return o @ w_o

def _trunk(x, c, hist_a, hist_f, kv_bufs, buf_widths, prompt, p):
    c_act = jax.nn.silu(c)
    kv_groups, new_bufs = None, None
    new_a, new_f = [], []
    for l in range(DEPTH):
        if l == N_A_LAYERS:
            kv_groups, new_bufs = _shared_kv(x, c_act, kv_bufs, buf_widths, prompt, p)
        mod = c_act @ p['w_mod'][l] + p['b_mod'][l]
        sh_m, sc_m, g_m, sh_f, sc_f, g_f = jnp.split(mod[:, None, :], N_MOD, axis=-1)
        h = _rmsnorm(x, p['norm_mix'][l]) * (1 + sc_m) + sh_m
        if l < N_A_LAYERS:
            out, nh = _conformer_conv(h, hist_a[l], p['a_w1'][l], p['a_b1'][l], p['a_dw'][l], p['a_dwb'][l],
                                      p['a_ln_g'][l], p['a_ln_b'][l], p['a_w2'][l], p['a_b2'][l])
            new_a.append(nh)
        else:
            lb = l - N_A_LAYERS
            out = _dilated_mixer(h, kv_groups, prompt, p['w_q'][lb], p['w_o'][lb], p['rel_bias'])
        x = x + g_m * out
        h = _rmsnorm(x, p['norm_ffn'][l]) * (1 + sc_f) + sh_f
        out, nh = _conv_ffn(h, hist_f[l], p['f_wup'][l], p['f_cw'][l], p['f_cb'][l], p['f_wdown'][l])
        new_f.append(nh)
        x = x + g_f * out
    return _rmsnorm(x, p['norm_f']), new_bufs, jnp.stack(new_a), jnp.stack(new_f)

def setup_inputs(seed: int = 0) -> dict:
    key = jax.random.key(seed)
    keys = iter(jax.random.split(key, 64))
    f32 = jnp.float32

    def nrm(shape, scale):
        return jax.random.normal(next(keys), shape, f32) * scale

    D = D_MODEL
    buf_w = [min(w, PAST_LEN) for w, _ in DIL_GROUPS]
    return {
        'x_prompt': nrm((BATCH, SEQ, D), 1.0),
        'x_sample': nrm((DEC_BATCH, DEC_SEQ, D), 1.0),
        'cache_kv_w128': nrm((DEC_BATCH, buf_w[0], 2, HEADS_PER_GROUP, HEAD_DIM), 1.0),
        'cache_kv_w512': nrm((DEC_BATCH, buf_w[1], 2, HEADS_PER_GROUP, HEAD_DIM), 1.0),
        'cache_kv_w2048': nrm((DEC_BATCH, buf_w[2], 2, HEADS_PER_GROUP, HEAD_DIM), 1.0),
        'state_conv_a': nrm((N_A_LAYERS, DEC_BATCH, CONV_A_WIDTH - 1, D), 0.5),
        'state_conv_ffn': nrm((DEPTH, DEC_BATCH, CONV_F_WIDTH - 1, 2 * D_FF), 1.0),
        'c_prompt': nrm((BATCH, D), 1.0),
        'c_sample': nrm((DEC_BATCH, D), 1.0),
        'w_mod': nrm((DEPTH, D, N_MOD * D), 0.5 * D ** -0.5),
        'b_mod': nrm((DEPTH, N_MOD * D), 0.02),
        'norm_mix': 1.0 + nrm((DEPTH, D), 0.05),
        'norm_ffn': 1.0 + nrm((DEPTH, D), 0.05),
        'a_w1': nrm((N_A_LAYERS, D, 2 * D), D ** -0.5),
        'a_b1': nrm((N_A_LAYERS, 2 * D), 0.02),
        'a_dw': nrm((N_A_LAYERS, CONV_A_WIDTH, D), CONV_A_WIDTH ** -0.5),
        'a_dwb': nrm((N_A_LAYERS, D), 0.02),
        'a_ln_g': 1.0 + nrm((N_A_LAYERS, D), 0.05),
        'a_ln_b': nrm((N_A_LAYERS, D), 0.02),
        'a_w2': nrm((N_A_LAYERS, D, D), D ** -0.5),
        'a_b2': nrm((N_A_LAYERS, D), 0.02),
        'w_mod_kv': nrm((D, 2 * D), 0.5 * D ** -0.5),
        'b_mod_kv': nrm((2 * D,), 0.02),
        'norm_kv': 1.0 + nrm((D,), 0.05),
        'w_kv': nrm((D, 2 * ATT_WIDTH), D ** -0.5),
        'w_q': nrm((N_B_LAYERS, D, ATT_WIDTH), D ** -0.5),
        'w_o': nrm((N_B_LAYERS, ATT_WIDTH, D), ATT_WIDTH ** -0.5),
        'rel_bias': nrm((N_BUCKETS, N_HEADS), 0.5),
        'f_wup': nrm((DEPTH, D, 2 * D_FF), D ** -0.5),
        'f_cw': nrm((DEPTH, CONV_F_WIDTH, 2 * D_FF), CONV_F_WIDTH ** -0.5),
        'f_cb': nrm((DEPTH, 2 * D_FF), 0.02),
        'f_wdown': nrm((DEPTH, D_FF, D), D_FF ** -0.5),
        'norm_f': 1.0 + nrm((D,), 0.05),
    }

def reference(x_prompt, x_sample, cache_kv_w128, cache_kv_w512, cache_kv_w2048, state_conv_a,
              state_conv_ffn, c_prompt, c_sample, w_mod, b_mod, norm_mix, norm_ffn, a_w1, a_b1, a_dw,
              a_dwb, a_ln_g, a_ln_b, a_w2, a_b2, w_mod_kv, b_mod_kv, norm_kv, w_kv, w_q, w_o, rel_bias,
              f_wup, f_cw, f_cb, f_wdown, norm_f):
    p = dict(w_mod=w_mod, b_mod=b_mod, norm_mix=norm_mix, norm_ffn=norm_ffn, a_w1=a_w1, a_b1=a_b1,
             a_dw=a_dw, a_dwb=a_dwb, a_ln_g=a_ln_g, a_ln_b=a_ln_b, a_w2=a_w2, a_b2=a_b2,
             w_mod_kv=w_mod_kv, b_mod_kv=b_mod_kv, norm_kv=norm_kv, w_kv=w_kv, w_q=w_q, w_o=w_o,
             rel_bias=rel_bias, f_wup=f_wup, f_cw=f_cw, f_cb=f_cb, f_wdown=f_wdown, norm_f=norm_f)
    kv_bufs = (cache_kv_w128, cache_kv_w512, cache_kv_w2048)
    buf_widths = tuple(b.shape[1] for b in kv_bufs)
    B = x_prompt.shape[0]
    hist_a0 = jnp.zeros((N_A_LAYERS, B, CONV_A_WIDTH - 1, D_MODEL), x_prompt.dtype)
    hist_f0 = jnp.zeros((DEPTH, B, CONV_F_WIDTH - 1, 2 * D_FF), x_prompt.dtype)
    y_prompt, kv_p, conv_a_p, conv_f_p = _trunk(x_prompt, c_prompt, hist_a0, hist_f0, None,
                                                buf_widths, True, p)
    y_sample, kv_s, conv_a_s, conv_f_s = _trunk(x_sample, c_sample, state_conv_a, state_conv_ffn,
                                                kv_bufs, buf_widths, False, p)
    return (y_prompt, y_sample, kv_p[0], kv_p[1], kv_p[2], conv_a_p, conv_f_p,
            kv_s[0], kv_s[1], kv_s[2], conv_a_s, conv_f_s)


_drawn_inputs = setup_inputs


def setup_inputs(seed=0):
    import zlib

    import numpy as np

    out = dict(_drawn_inputs(seed))
    spreads = {}
    factors = {'a_b1': 2.779,
     'a_dwb': 7.661,
     'a_ln_g': 5.22,
     'a_ln_b': 8.0,
     'a_b2': 8.0,
     'rel_bias': 5.342,
     'f_cb': 7.571}
    for name, (base, spread) in spreads.items():
        noise = np.random.default_rng([zlib.crc32(name.encode()), seed]).standard_normal(out[name].shape)
        drawn = base * np.exp(spread * noise) if base else spread * noise
        out[name] = __import__('jax').numpy.asarray(drawn.astype(out[name].dtype))
    for name, factor in factors.items():
        out[name] = (out[name] * factor).astype(out[name].dtype)
    return out
```

```python
from contextlib import ExitStack

import numpy as np
import concourse.bass as bass
from concourse import mybir

F = mybir.dt.float32
R = mybir.dt.float32r
ALU = mybir.AluOpType
ACT = mybir.ActivationFunctionType
AX = mybir.AxisListType.X

P = 128
D = 1024
KD = D // P
TP = 1024
NS, TS_ = 8, 4
TSAM = NS * TS_
T = TP + TSAM
NC = 3
CW = T // NC
DFF = 2816
NJ = DFF // P
NG = NJ // 2
CA = 31
HA = CA - 1
SPAN = 128
DIL = (1, 4, 16)
EPS, LN_EPS = 1e-6, 1e-5
NEG = -1e30

UNIT = 1024
A0, A1, D0, D1 = range(4)
UC = TP + 6 * NS
UL = UC + 6
FL = HA + TP + (HA + TS_) * NS
FS = HA + TP
FSEG = HA + TS_

NMOD = 112
P_BM = 0
P_NM0, P_NF0, P_NKV, P_NM1, P_NF1, P_NFIN = (NMOD + 8 * i for i in range(6))
P_B1A = P_NFIN + 8
P_B1G = P_B1A + 8
P_DWB, P_LNG, P_LNB, P_B2 = (P_B1G + 8 * (i + 1) for i in range(4))
P_DW = P_B2 + 8
P_END = P_DW + 8 * CA
Q_SHM0, Q_SCM0, Q_GM0, Q_SHF0, Q_SCF0, Q_GF0, Q_SHKV, Q_SCKV, Q_SHM1, Q_SCM1, Q_GM1, Q_SHF1, Q_SCF1, Q_GF1 = (
    8 * i for i in range(14))

PHASES = {}
LAND, SPLIT, FIRST = [0] * 4, [0] * 4, 0
for _name, _uses, _raw in (
        ("mod", (4, 4, 4, 4), 0), ("w1", (8, 8, 48, 48), 0), ("w2", (2, 2, 2, 2), 0),
        ("ffn0", (22, 22, 11, 11), 0), ("kv", (3, 3, 3, 3), 0), ("q", (3, 3, 0, 0), 0),
        ("att", (9, 9, 9, 9), 1), ("wo", (2, 2, 2, 2), 0), ("ffn1", (22, 22, 11, 11), 0)):
    PHASES[_name] = (FIRST, tuple(LAND), tuple(SPLIT))
    for _s in range(4):
        LAND[_s] += _uses[_s]
        SPLIT[_s] += 0 if _raw else _uses[_s]
    FIRST += 0 if _raw else sum(_uses)
N_UNITS = FIRST
N_ATT = 36


ARENA = 212800


def program(nc, ins, outs):
    with ExitStack() as ctx:
        enter = ctx.enter_context
        enter(nc.sbuf_tensor("arena", [P, ARENA // 4], F))
        start = nc.sbuf_base - ARENA

        def at(name, shape, dt, off):
            return nc.alloc_sbuf_tensor_at(name, shape, dt, offset=start + off, align_bytes=8)

        o = 0
        x = at("x", [P, KD, T], F, o); o += KD * T * 4
        o_h = o
        h_hi = at("h_hi", [P, KD, T], R, o_h)
        h_lo = at("h_lo", [P, KD, T], R, o_h + KD * T * 4)
        o += 2 * KD * T * 4
        o_split = o
        w_hi = [at(f"w_hi{s}", [P, UNIT], R, o + 8192 * s) for s in range(4)]
        w_lo = [at(f"w_lo{s}", [P, UNIT], R, o + 8192 * s + 4096) for s in range(4)]
        o += 4 * 8192
        w_raw = [at(f"w_raw{s}", [P, UNIT], F, o + 4096 * s) for s in range(4)]
        o += 4 * 4096
        o_f = o
        z_hi = [at(f"z_hi{i}", [P, T], R, o_f + 8448 * i) for i in range(2)]
        z_lo = [at(f"z_lo{i}", [P, T], R, o_f + 8448 * i + 4224) for i in range(2)]
        u = [at(f"u{i}", [P, UL], F, o_f + 16896 + UL * 4 * i) for i in range(2)]
        cv = [at(f"cv{i}", [P, UC], F, o_f + 16896 + UL * 8 + UC * 4 * i) for i in range(2)]
        ycv = at("ycv", [P, KD, T], F, o_f)
        tmp = [at(f"tmp{i}", [P, T], F, o_f + 4224 * i) for i in range(2)]
        kst = [at(f"kst{i}", [P, T], F, o_f + 8448 + 4224 * i) for i in range(2)]
        sq = [at(f"sq{i}", [P, T], F, o_f + 25600 + 4224 * i) for i in range(2)]
        o += 34112
        o_t = o
        tb = [at(f"tb{i}", [P, T], F, o_t + 4224 * i) for i in range(2)]
        rstd = at("rstd", [P, T], F, o_t)
        sg = at("sg", [P, T], F, o_t)
        ysum = at("ysum", [P, T], F, o_t + 4224)
        o += 8448
        o_m = o
        full = [at(f"full{i}", [P, FL], F, o_m + 5312 * i) for i in range(2)]
        mu = at("mu", [P, T], F, o_m)
        ysq = at("ysq", [P, T], F, o_m + 4224)
        hist = at("hist", [P, 2 * NJ, 16], F, o_m)
        ostate = at("ostate", [P, 2 * NJ, 18], F, o_m + 2816)
        cwb = at("cwb", [P, 2 * NJ, 4], F, o_m + 5984)
        acc = at("acc", [P, T], F, o_m + 6720)
        vst = [at(f"vst{i}", [P, 256], F, o_m + 1024 * i) for i in range(4)]
        o += 10960
        mod = at("mod", [P, NMOD, 9], F, o); o += NMOD * 9 * 4
        prm = at("prm", [P, P_END], F, o); o += P_END * 4
        o_c = o
        cact = at("cact", [P, KD, 10], F, o)
        c_spl = at("c_spl", [P, KD, 20], R, o_c + 1024); o = o_c + 1664
        gain = at("gain", [P, KD, 9], F, o); o += 288
        b2g = at("b2g", [P, KD], F, o); o += 32
        ident = at("ident", [P, P], F, o); o += 512
        ones = at("ones", [P, 2], F, o); o += 32
        cols = at("cols", [P, 6, 9], F, o); o += 224
        tsam = at("tsam", [P, KD, TSAM], F, o_c)
        scr = tsam[:, :, :].rearrange("p k n -> p (k n)")[:, 0:NS * CA].rearrange("p (n w) -> p n w", w=CA)
        assert o <= ARENA, o

        kt = at("kt", [P, 6, T], F, o_h)
        v_sb = [at(f"v{g}", [P, 8, 256], F, o_h + 25344 + 8192 * g) for g in range(3)]
        lg = [at(f"logits{i}", [P, 8, 256], F, o_h + 49920 + 8192 * i) for i in range(2)]
        stat = at("stat", [P, 3, 12, 8], F, o_h + 66304)
        rsum = at("rsum", [P, 12, 8], F, o_c + 1024)
        qt = at("qt", [P, 6, T], F, o_f)
        btab = at("btab", [P, 4, 2, 256], F, o_f + 25344)
        o_hi = at("o_hi", [P, 6, T], R, o_h)
        o_lo = at("o_lo", [P, 6, T], R, o_f)
        lse = [at(f"lse{g}", [P, TP], F, o_split + 4096 * g) for g in range(3)]
        top = at("top", [P, TP], F, o_split + 12288)
        rz = at("rz", [P, TP], F, o_split + 16384)
        orow = [at(f"orow{g}", [P, TP], F, o_split + 20480 + 4096 * g) for g in range(3)]
        pt = [at(f"pt{i}", [P, 512], F, o_m + 2048 * i) for i in range(2)]
        s_sb = at("s_sb", [P, 384], F, o_m + 4096)
        sn_sb = at("sn_sb", [TSAM, 384], F, o_m + 5632)
        bsam = at("bsam", [P, 3, 160], F, o_m + 7168)
        lsam = at("lsam", [P, 3, 160], F, o_h + 49920 + 8192)
        qd = at("qd", [P, 6, TSAM, 2], F, o_t)
        vn = at("vn", [TSAM, 768], F, o_t + 1536)
        pc = at("pc", [P, 384], F, o_t + 4608)
        pn = at("pn", [TSAM, 384], F, o_t + 6144)
        osam = at("osam", [P, 6, TSAM], F, o_t + 7680)
        zeros = at("zeros", [P, UNIT], F, o_f + 16896)

        bank = [enter(nc.psum_tensor(f"bank{i}", [P, 512], F)) for i in range(8)]

        def sem(name):
            return enter(nc.semaphore(name))

        landed = [sem(f"landed{s}") for s in range(4)]
        hi_done = [sem(f"hi_done{s}") for s in range(4)]
        split = [sem(f"split{s}") for s in range(4)]
        used = [sem(f"used{s}") for s in range(4)]
        job_free = [sem(f"job_free{b}") for b in range(2)]
        mod_free = [sem(f"mod_free{b}") for b in range(2)]
        consts = sem("consts")
        params = [sem(f"params{i}") for i in range(3)]
        xload = [sem(f"xload{i}") for i in range(2)]

        def n_split(ph, s, k):
            return PHASES[ph][2][s] + k

        def n_land(ph, s, k):
            return PHASES[ph][1][s] + k

        def fetch(e, ph, s, n, k, first=False):
            if not first:
                e.wait_ge(split[s], n_split(ph, s, k))
            n = n + PHASES[ph][0]
            src = ins["ws"][n] if isinstance(n, int) else ins["ws"][bass.ds(n, 1)].rearrange("o p n -> p (o n)")
            e.dma_start(w_raw[s][:, :], src).then_inc(landed[s], 16)

        def pool_wait(e, s, n):
            e.wait_ge(s, n)
            if not isinstance(n, int):
                e.nop(nofuse=True)

        def put_hi(e, ph, s, k, first=False, act=False):
            e.wait_ge(landed[s], 16 * n_land(ph, s, k) + 16)
            if act:
                if not first:
                    e.wait_ge(used[s], n_split(ph, s, k))
                nc.scalar.copy(w_hi[s][:, :], w_raw[s][:, :]).then_inc(hi_done[s], 1)
            else:
                pool_wait(e, used[s], n_split(ph, s, k))
                e.tensor_scalar(w_hi[s][:, :], w_raw[s][:, :], 1.0, None, ALU.mult).then_inc(hi_done[s], 1)

        def put_lo(e, ph, s, k):
            pool_wait(e, hi_done[s], n_split(ph, s, k) + 1)
            e.tensor_tensor(w_lo[s][:, :], w_raw[s][:, :], w_hi[s][:, :].bitcast(F), ALU.subtract).then_inc(split[s], 1)

        def put(e, ph, s, k):
            put_hi(e, ph, s, k)
            put_lo(e, ph, s, k)

        def product(e, ph, s, k, b, job, hi, lo, nk=KD, ready=None, first=False):
            e.wait_ge(split[s], n_split(ph, s, k) + 1)
            if not first:
                e.wait_ge(job_free[b], job)
            for kk in range(nk):
                if ready is not None:
                    e.wait_ge(ready[0], ready[1] + kk + 1)
                for q, (w, a) in enumerate(((w_hi, hi), (w_hi, lo), (w_lo, hi))):
                    for c in range(NC):
                        mm = e.matmul(bank[3 * b + c][:, 0:CW], w[s][:, kk * P:(kk + 1) * P],
                                      a[:, kk, c * CW:(c + 1) * CW], start=(kk == 0 and q == 0),
                                      stop=(kk == nk - 1 and q == 2))
            mm.then_inc(used[s], 1)

        def modulate(e, ph, s, k, b, n, first=False):
            e.wait_ge(split[s], n_split(ph, s, k) + 1)
            if not first:
                e.wait_ge(mod_free[b], n)
            for kk in range(KD):
                w = w_hi[s][:, kk * P:(kk + 1) * P]
                e.matmul(bank[6 + b][:, 0:10], w, c_spl[:, kk, 0:10], start=(kk == 0), stop=False)
                e.matmul(bank[6 + b][:, 0:10], w, c_spl[:, kk, 10:20], start=False, stop=False)
                mm = e.matmul(bank[6 + b][:, 0:10], w_lo[s][:, kk * P:(kk + 1) * P], c_spl[:, kk, 0:10],
                              start=False, stop=(kk == KD - 1))
            mm.then_inc(used[s], 1)

        def take_mod(e, ph, s, k, b, q):
            e.wait_ge(used[s], n_split(ph, s, k) + 1)
            qs = slice(q, q + 1) if isinstance(q, int) else bass.ds(q, 1)
            nc.scalar.activation(mod[:, qs, :].rearrange("p o n -> p (o n)"), bank[6 + b][:, 0:9], ACT.Identity,
                                 bias=prm[:, qs]).then_inc(mod_free[b], 1)

        def col(base, m):
            return prm[:, base + m:base + m + 1] if isinstance(m, int) else prm[:, bass.ds(m + base, 1)]

        class Chain:

            def __init__(self, e, s, base=0):
                self.e, self.s, self.n = e, s, base

            def __call__(self, instruction):
                instruction.then_inc(self.s, 1)
                self.n = self.n + 1
                self.e.wait_ge(self.s, self.n)

        col_sum, col_val, col_root, col_inv, wide = (sem(f"norm_{x}") for x in ("sum", "val", "root", "inv", "wide"))
        wide_sb = sem("norm_wide_sb")
        sq_done, sq_added = sem("sq_done"), sem("sq_added")
        h_pre, h_aff, h_hi_done, h_ready = (sem(f"h_{x}") for x in ("pre", "affine", "hi_done", "ready"))
        x_final = sem("x_final")
        dve = sem("dve")
        act_own = sem("act_own")

        def pe_sum(e, rs, src, need):
            e.wait_ge(*need)
            for t in range(9):
                lo = t * P if t < 8 else T - P
                mm = e.matmul(bank[6][:, t:t + 1], src[:, lo:lo + P], ones[:, 0:1], start=True, stop=True)
            mm.then_inc(col_sum, 1)

        def pe_wide(e, c, need):
            e.wait_ge(*need)
            for t in range(9):
                rhs = ident[:, :] if t < 8 else ident[:, P - TSAM:P]
                out = bank[t // 4][:, (t % 4) * P:(t % 4 + 1) * P] if t < 8 else bank[2][:, 0:TSAM]
                mm = e.matmul(out, cols[:, c, t:t + 1].to_broadcast([P, P]), rhs, start=True, stop=True)
            mm.then_inc(wide, 1)

        def act_wide(e, rs, dst):
            e.wait_ge(wide, rs + 1)
            for b, w in ((0, 512), (1, 512), (2, TSAM)):
                last = nc.scalar.copy(dst[:, 512 * b:512 * b + w], bank[b][:, 0:w])
            last.then_inc(wide_sb, 1)

        def act_root(e, r):
            e.wait_ge(col_val, r + 1)
            nc.scalar.activation(cols[:, 2, :], cols[:, 0, :], ACT.Sqrt).then_inc(col_root, 1)

        def dve_inverse_root(e, ch, r, rs, eps):
            e.wait_ge(col_sum, rs + 1)
            e.tensor_scalar(cols[:, 0, :], bank[6][:, 0:9], 1.0 / D, eps, ALU.mult, ALU.add).then_inc(col_val, 1)
            e.wait_ge(col_root, r + 1)
            ch(e.reciprocal(cols[:, 1, :], cols[:, 2, :]))
            ch(e.tensor_tensor(cols[:, 3, :], cols[:, 1, :], cols[:, 1, :], ALU.mult))
            ch(e.tensor_tensor(cols[:, 3, :], cols[:, 3, :], cols[:, 0, :], ALU.mult))
            ch(e.tensor_scalar(cols[:, 3, :], cols[:, 3, :], -0.5, 1.5, ALU.mult, ALU.add))
            e.tensor_tensor(cols[:, 4, :], cols[:, 1, :], cols[:, 3, :], ALU.mult).then_inc(col_inv, 1)

        def act_square(e, r, k, src, buf, need):
            e.wait_ge(*need)
            if k >= 2:
                e.wait_ge(sq_added, 8 * r + k - 1)
            nc.scalar.activation(buf[k % 2][:, :], src[:, k, :], ACT.Square).then_inc(sq_done, 1)

        def dve_add_square(e, r, k, buf, into):
            e.wait_ge(sq_done, 8 * r + k + 1)
            if k == 0:
                e.tensor_copy(into[:, :], buf[0][:, :]).then_inc(sq_added, 1)
            else:
                e.wait_ge(sq_added, 8 * r + k)
                e.tensor_tensor(into[:, :], into[:, :], buf[k % 2][:, :], ALU.add).then_inc(sq_added, 1)

        def as_seq(a):
            return a.rearrange("p k (n t) -> p k n t", t=TS_)

        def per_seq(a):
            return a.unsqueeze(3).to_broadcast([P, KD, NS, TS_])

        def dve_gain(e, ch, p_gain, q_scale):
            ch(e.tensor_scalar(gain[:, :, :], mod[:, q_scale:q_scale + 8, :], 1.0, None, ALU.add))
            ch(e.tensor_tensor(gain[:, :, :], gain[:, :, :],
                               prm[:, p_gain:p_gain + 8].unsqueeze(2).to_broadcast([P, KD, 9]), ALU.mult))

        def dve_ada(e, ch, a, q_shift, buf):
            ch(e.tensor_tensor(tsam[:, :, :], x[:, :, TP:T], rstd[:, TP:T].unsqueeze(1).to_broadcast([P, KD, TSAM]),
                               ALU.mult))
            ch(e.tensor_tensor(as_seq(tsam), as_seq(tsam), per_seq(gain[:, :, 1:9]), ALU.mult))
            ch(e.tensor_tensor(as_seq(tsam), as_seq(tsam), per_seq(mod[:, q_shift:q_shift + 8, 1:9]), ALU.add))
            for k in range(KD):
                if k >= 2:
                    e.wait_ge(h_ready, 8 * a + k - 1)
                e.tensor_copy(buf[k % 2][:, TP:T], tsam[:, k, :])
                e.tensor_tensor(buf[k % 2][:, 0:TP], x[:, k, 0:TP], rstd[:, 0:TP], ALU.mult).then_inc(h_pre, 1)

        def act_ada(e, a, q_shift, buf, n_aff):
            for k in range(KD):
                e.wait_ge(h_pre, 8 * a + k + 1)
                nc.scalar.activation(buf[k % 2][:, 0:TP], buf[k % 2][:, 0:TP], ACT.Identity,
                                     scale=gain[:, k, 0:1], bias=mod[:, q_shift + k, 0:1]).then_inc(h_aff, 1)
                e.wait_ge(h_aff, 8 * n_aff + k + 1)
                nc.scalar.copy(h_hi[:, k, :], buf[k % 2][:, :]).then_inc(h_hi_done, 1)

        def pool_lo(e, a, buf):
            for k in range(KD):
                e.wait_ge(h_hi_done, 8 * a + k + 1)
                e.tensor_tensor(h_lo[:, k, :], buf[k % 2][:, :], h_hi[:, k, :].bitcast(F), ALU.subtract
                                ).then_inc(h_ready, 1)

        def act_result(e, need, b, tbuf, gate0, bias0, bias1, free_need):
            e.wait_ge(*need)
            if free_need is not None:
                e.wait_ge(x_final, free_need)
            kw = dict(bias=bias0) if bias0 is not None else {}
            for c in range(NC):
                w = CW if c < 2 else TP - 2 * CW
                nc.scalar.activation(tbuf[:, c * CW:c * CW + w], bank[3 * b + c][:, 0:w], ACT.Identity,
                                     scale=gate0, **kw)
            kw = dict(bias=bias1) if bias1 is not None else {}
            nc.scalar.activation(tbuf[:, TP:T], bank[3 * b + 2][:, TP - 2 * CW:CW], ACT.Identity,
                                 **kw).then_inc(job_free[b], 1)

        def dve_result(e, ch, need, tbuf, gates, xm):
            e.wait_ge(*need)
            ts = tbuf[:, TP:T].rearrange("p (n t) -> p n t", t=TS_)
            ch(e.tensor_tensor(ts, ts, gates.unsqueeze(2).to_broadcast([P, NS, TS_]), ALU.mult))
            e.tensor_tensor(xm, xm, tbuf[:, :], ALU.add).then_inc(x_final, 1)

        c_sem, c_lo, mean_col = sem("c_hi"), sem("c_lo"), sem("mean_col")
        hist_in, cap_out = [sem(f"hist_in{i}") for i in range(2)], [sem(f"cap_out{i}") for i in range(2)]
        conv_done, conv_y, ln_dve = sem("conv_done"), sem("conv_y"), sem("ln_dve")
        centred = sem("centred")
        FF = [dict(conv=[sem(f"f{l}_conv{w}") for w in range(2)], op1=[sem(f"f{l}_op1{w}") for w in range(2)],
                   silu=sem(f"f{l}_silu"), mul=sem(f"f{l}_mul"), zh=sem(f"f{l}_zh"), zl=sem(f"f{l}_zl"),
                   dn=sem(f"f{l}_down"), load=sem(f"f{l}_load"), load2=sem(f"f{l}_load2"), state=sem(f"f{l}_state"), zero=sem(f"f{l}_zero"),
                   dve=sem(f"f{l}_dve")) for l in range(2)]
        copies = sem("copies")
        out_sem, y_ready = sem("out_sem"), sem("y_ready")
        JB = {"w1": 0, "w2": 8, "ffn0": 12, "k": 78, "q": 81, "wo": 84, "ffn1": 88}
        XB = {"w2": 0, "ffn0": 8, "wo": 96, "ffn1": 104}

        def cache_rows(g, n):
            w = SPAN * DIL[g] * 512
            cut = TS_ * 512
            return ins[f"cache{g}"][bass.ds(n, 1)].rearrange("o m -> (o m)")[cut:w].rearrange("(a b) -> a b", a=P)

        def sp_ffn(e, l):
            ph = f"ffn{l}"
            ff = FF[l]
            need = (h_pre, 8 * (2 if l == 0 else 5) + 8)

            def ups(n, k):
                for w in range(2):
                    fetch(e, ph, w, n + w, k)

            ups(0, 0)
            e.wait_ge(*need)
            e.dma_start(cwb[:, :, :], ins["cwb"][l]).then_inc(ff["load"], 16)
            e.dma_start(hist[:, :, :], ins["hist_f"][l]).then_inc(ff["load2"], 16)
            ups(2, 1)
            def group(f):
                ups(6 * f - 2, 2 * f)
                for s in (D0, D1):
                    fetch(e, ph, s, 6 * f + s - D0, f - 1)
                ups(6 * f + 2, 2 * f + 1)

            if l == 0:
                with e.Fori(1, 1 + NS) as f:
                    group(f)
                    for g in range(3):
                        e.dma_start(outs[f"kvs{g}"][bass.ds(f - 1, 1)].rearrange("o (a b) -> (o a) b", a=P),
                                    cache_rows(g, f - 1)).then_inc(copies, 16)
                with e.Fori(1 + NS, NG) as f:
                    group(f)
            else:
                with e.Fori(1, NG) as f:
                    group(f)
            for s in (D0, D1):
                fetch(e, ph, s, 6 * NG - 2 + s - D0, NG - 1)

        kst_out, vst_out = [sem(f"kst_out{i}") for i in range(2)], [sem(f"vst_out{i}") for i in range(4)]
        v_done, v_free, cfo_out = sem("v_done"), [sem(f"v_free{i}") for i in range(2)], [sem(f"cfo_out{i}") for i in range(2)]
        zset, zero_out = sem("zeros_set"), sem("zero_out")
        att_in = [sem(f"att_in{i}") for i in range(8)]
        b_in = [sem(f"bias_in{i}") for i in range(4)]
        att_used = [sem(f"att_used{s}") for s in range(4)]
        at_ = {x: sem(f"att_{x}") for x in (
            "qd", "sc", "ss", "st", "smax", "sexp", "sp", "sb", "spc", "osam", "s_done", "s_free", "nm", "exp", "p", "t_done",
            "pt", "pv", "o_free", "ln", "lse", "lb", "ls", "sub", "e", "z", "hi", "o_ready", "chain")}
        PREV = [[b > 0 for b in range(8)], [b % 2 == 1 for b in range(8)], [False] * 8]

        def branch_view(a, g, lo, hi):
            d = DIL[g]
            return a[:, 0:TP].rearrange("p (r i) -> p r i", r=d)[:, :, lo // d:hi // d]

        def as_residues(a, g):
            return a.rearrange("p (i r) -> p r i", r=DIL[g])

        block = enter(nc.Block())

        @block.sync
        def _(e):
            e.dma_start(cact[:, :, :], ins["ct"]).then_inc(params[0], 16)
            e.dma_start(prm[:, :], ins["prm"]).then_inc(params[1], 16)
            for i in range(4):
                for s in range(4):
                    fetch(e, "mod", s, 4 * i + s, i, first=(i == 0))
                if i == 0:
                    for hf in range(2):
                        e.dma_start(x[:, 4 * hf:4 * hf + 4, :], ins["xt"][:, 4 * hf:4 * hf + 4, :]).then_inc(xload[hf], 16)
                    e.dma_start(ident[:, :], ins["ident"]).then_inc(params[2], 16)
                    for mm in range(2):
                        e.dma_start(full[mm][:, FS:FL].rearrange("p (n r) -> p n r", r=FSEG)[:, :, 0:HA],
                                    ins["hist_a"][mm].rearrange("p (n r) -> p n r", r=HA)).then_inc(hist_in[mm], 16)

            e.wait_ge(zset, 1)
            for r in range(4):
                e.dma_start(outs["kvz"][r], zeros[:, :]).then_inc(zero_out, 16)

            def state_out(m, b, i):
                e.wait_ge(job_free[1], m + 1)
                cap = outs["cap"][m] if isinstance(m, int) else outs["cap"][bass.ds(m, 1)].rearrange("o p n -> p (o n)")
                e.dma_start(cap[:, 0:HA], full[b][:, TP:TP + HA]).then_inc(cap_out[b], 16)
                e.wait_ge(cap_out[b], 32 * i + 16)
                e.dma_start(cap[:, HA:HA * 9].rearrange("p (n r) -> p n r", r=HA),
                            full[b][:, FS:FL].rearrange("p (n r) -> p n r", r=FSEG)[:, :, TS_:FSEG]).then_inc(cap_out[b], 16)
                e.wait_ge(cap_out[b], 32 * i + 32)

            def w1_units(i):
                for mm in range(2):
                    k = 2 * i + mm
                    fetch(e, "w1", A0, 14 * k, k)
                    fetch(e, "w1", A1, 14 * k + 1, k)
                    for j in range(12):
                        fetch(e, "w1", D0 + j % 2, 14 * k + 2 + j, 6 * k + j // 2)
                        if j == 5 and not isinstance(i, int):
                            state_out(k - 2, mm, i - 1)
                            e.wait_ge(conv_done, k - 1)
                            e.dma_start(full[mm][:, FS:FL].rearrange("p (n r) -> p n r", r=FSEG)[:, :, 0:HA],
                                        ins["hist_a"][bass.ds(k, 1)].rearrange("o p (n r) -> p (o n) r", r=HA)
                                        ).then_inc(hist_in[mm], 16)

            w1_units(0)
            with e.Fori(1, 4) as i:
                w1_units(i)
            for mm in range(2):
                state_out(6 + mm, mm, 3)
            for r in range(2):
                for s in range(4):
                    fetch(e, "w2", s, 4 * r + s, r)
            sp_ffn(e, 0)
            for ss in ((A0, A1, 0), (D0, D1, 0), (A0, A1, 1), (D0, D1, 1), (A0, A1, 2)):
                for s in ss[:2]:
                    fetch(e, "kv", s, 2 * ss[2] + s if s < D0 else 6 + 2 * ss[2] + s - D0, ss[2])
                if ss == (A0, A1, 0):
                    e.wait_ge(FF[0]["state"], 2 * NJ)
                    e.dma_start(outs["cfo"][0], ostate[:, :, :]).then_inc(cfo_out[0], 16)
            for c in range(6):
                e.wait_ge(job_free[c % 2], JB["k"] + c // 2 + 1)
                e.dma_start(outs["kt"][c], kst[c % 2][:, :]).then_inc(kst_out[c % 2], 16)

            def v_store(g):
                for t in range(9):
                    n = 9 * g + t
                    e.wait_ge(v_free[n % 2], n // 2 + 1)
                    sr = vst[n % 4][:, :] if t < 8 else vst[n % 4][P - TSAM:P, :]
                    e.dma_start(outs["v"][t * P:t * P + (P if t < 8 else TSAM), 256 * g:256 * g + 256], sr
                                ).then_inc(vst_out[n % 4], 16)

            v_store(0)
            for s in (D0, D1):
                fetch(e, "kv", s, 10 + s - D0, 2)
            v_store(1)
            for s in (A0, A1):
                fetch(e, "q", s, s, 0)
            v_store(2)
            for k in range(1, 3):
                for s in (A0, A1):
                    fetch(e, "q", s, 2 * k + s, k)
            for s in (A0, A1):
                e.wait_ge(used[s], n_split("q", s, 2) + 1)
            for b in range(2):
                e.wait_ge(kst_out[b], 48)
            for b in range(4):
                e.wait_ge(vst_out[b], 16 * (7 if b < 3 else 6))
            e.dma_start(kt[:, :, :], outs["kt"].rearrange("c p t -> p c t")).then_inc(att_in[0], 16)
            v = outs["v"]
            e.dma_start(v_sb[0][:, :, :], v[0:TP, 0:256].rearrange("(b p) n -> p b n", p=P)).then_inc(att_in[1], 16)
            e.dma_start(vn[:, :], v[TP:T, :]).then_inc(att_in[2], 16)
            e.dma_start(bsam[:, :, :], ins["bias_s"]).then_inc(att_in[3], 16)

            def load_bias(n):
                e.dma_start(btab[:, n % 4, :, :], ins["bias_p"][n]).then_inc(b_in[n % 4], 16)

            for n in range(4):
                load_bias(n)

            def att_unit(n):
                s, k = n % 4, n // 4
                if k == 0:
                    e.wait_ge(split[s], n_split("att", s, 0))
                else:
                    e.wait_ge(att_used[s], k)
                e.dma_start(w_raw[s][:, :], ins["att"][n]).then_inc(landed[s], 16)

            for n in range(4):
                att_unit(n)
            e.dma_start(v_sb[1][:, :, :].rearrange("p (r b) n -> p r b n", r=4),
                        v[0:TP, 256:512].rearrange("(b p r) n -> p r b n", b=2, r=4)).then_inc(att_in[4], 16)
            for r in range(2):
                e.dma_start(v_sb[2][64 * r:64 * r + 64, :, :],
                            v[0:TP, 512:768].rearrange("(i b r) n -> r i b n", b=8, r=2)[r]).then_inc(att_in[5 + r], 16)
            for n in range(4, 22):
                att_unit(n)
            for n in (4, 5):
                e.wait_ge(at_["nm"], 2 * (n - 4) + 2)
                load_bias(n)
            for n in range(22, N_ATT):
                att_unit(n)
            for s in range(4):
                e.wait_ge(att_used[s], 9)
                fetch(e, "wo", s, s, 0)
            for s in range(4):
                fetch(e, "wo", s, 4 + s, 1)
            sp_ffn(e, 1)
            e.wait_ge(FF[1]["state"], 2 * NJ)
            e.dma_start(outs["cfo"][1], ostate[:, :, :]).then_inc(cfo_out[1], 16)
            for k in range(KD):
                e.wait_ge(y_ready, k + 1)
                e.dma_start(outs["yt"][:, k, :], x[:, k, :]).then_inc(out_sem, 16)
            e.wait_ge(out_sem, 16 * KD)
            e.wait_ge(copies, 16 * 3 * NS)
            for b in range(2):
                e.wait_ge(cfo_out[b], 16)
                e.wait_ge(cap_out[b], 128)
            e.wait_ge(zero_out, 64)

        def pool_ffn(e, l):
            ph, ff = f"ffn{l}", FF[l]

            def z_lo_part(j, zi):
                pool_wait(e, ff["zh"], j + 1)
                e.tensor_tensor(z_lo[zi][:, 0:TP], cv[1][:, 0:TP], z_hi[zi][:, 0:TP].bitcast(F), ALU.subtract)
                e.tensor_tensor(z_lo[zi][:, TP:T].rearrange("p (n t) -> p n t", t=TS_), cv_sam(cv[1]),
                                z_hi[zi][:, TP:T].bitcast(F).rearrange("p (n t) -> p n t", t=TS_), ALU.subtract
                                ).then_inc(ff["zl"], 1)

            for k in range(2):
                for s in (A0, A1):
                    put(e, ph, s, k)
                if k == 1:
                    z_lo_part(0, 0)
            with e.Fori(1, NG) as f:
                for s in (A0, A1):
                    put(e, ph, s, 2 * f)
                z_lo_part(2 * f - 1, 1)
                for s in (D0, D1):
                    put(e, ph, s, f - 1)
                for s in (A0, A1):
                    put(e, ph, s, 2 * f + 1)
                z_lo_part(2 * f, 0)
            z_lo_part(NJ - 1, 1)
            for s in (D0, D1):
                put(e, ph, s, NG - 1)

        def cv_sam(c):
            return c[:, TP:TP + 6 * NS].rearrange("p (n r) -> p n r", r=6)[:, :, 2:2 + TS_]

        @block.gpsimd
        def _(e):
            e.memset(zeros[:, :], 0.0).then_inc(zset, 1)
            for i in range(4):
                for s in range(4):
                    put_lo(e, "mod", s, i)
            pool_lo(e, 0, tmp)
            with e.Fori(0, 4) as i:
                for mm in range(2):
                    k = 2 * i + mm
                    put(e, "w1", A0, k)
                    put(e, "w1", A1, k)
                    for j in range(12):
                        if j < 2:
                            put_hi(e, "w1", D0 + j % 2, 6 * k + j // 2)
                        put_lo(e, "w1", D0 + j % 2, 6 * k + j // 2)
            for s in range(4):
                put(e, "w2", s, 0)
            pool_lo(e, 1, (mu, ysq))
            for s in range(4):
                put(e, "w2", s, 1)
            pool_lo(e, 2, tmp)
            pool_ffn(e, 0)
            for s in range(4):
                put(e, "kv", s, 0)
            pool_lo(e, 3, tmp)
            for s in (A0, A1):
                put(e, "kv", s, 1)
            for s in (A0, A1):
                put(e, "kv", s, 2)
            for k in (1, 2):
                for s in (D0, D1):
                    put(e, "kv", s, k)
            for s in (A0, A1):
                put(e, "q", s, 0)
            pool_lo(e, 4, tmp)
            for k in range(1, 3):
                for s in (A0, A1):
                    put(e, "q", s, k)
            e.wait_ge(at_["o_ready"], 8)
            for s in range(4):
                put(e, "wo", s, 0)
            for s in range(4):
                put(e, "wo", s, 1)
            pool_lo(e, 5, tmp)
            pool_ffn(e, 1)

        def act_ffn(e, l, q_gate, after_last):
            ph, ff, jb, xb = f"ffn{l}", FF[l], JB[f"ffn{l}"], XB[f"ffn{l}"]

            def up(j, w, job, first):
                ch = j + NJ * w
                cs = slice(ch, ch + 1) if isinstance(ch, int) else bass.ds(ch, 1)
                e.wait_ge(used[A0 + w], n_split(ph, A0 + w, j) + 1)
                if not first:
                    e.wait_ge(ff["conv"][w], j)
                segs = u[w][:, 2 + TP:2 + UC].rearrange("p (n r) -> p n r", r=6)
                nc.scalar.copy(segs[:, :, 0:2], hist[:, cs, :].rearrange("p o (n r) -> p (o n) r", r=2))
                for c in range(NC):
                    w_ = CW if c < 2 else TP - 2 * CW
                    nc.scalar.copy(u[w][:, 2 + c * CW:2 + c * CW + w_], bank[3 * w + c][:, 0:w_])
                nc.scalar.copy(segs[:, :, 2:6], bank[3 * w + 2][:, TP - 2 * CW:CW].rearrange("p (n t) -> p n t", t=TS_)
                               ).then_inc(job_free[w], 1)
                e.wait_ge(job_free[w], job + 1)
                if not first:
                    if w == 0:
                        e.wait_ge(ff["mul"], j)
                    else:
                        e.wait_ge(ff["zl"], j)
                nc.scalar.activation(cv[w][:, :], u[w][:, 0:UC], ACT.Identity,
                                     scale=cwb[:, cs, 0:1].rearrange("p o n -> p (o n)"),
                                     bias=cwb[:, cs, 3:4].rearrange("p o n -> p (o n)")).then_inc(ff["op1"][w], 1)
                nc.scalar.copy(ostate[:, cs, :].rearrange("p o (n r) -> p (o n) r", r=2),
                               u[w][:, TP:TP + 54].rearrange("p (n r) -> p n r", r=6)[:, :, 0:2]
                               ).then_inc(ff["state"], 1)

            def ups(j, job, first=False):
                for w in range(2):
                    up(j, w, job, first)
                e.wait_ge(ff["conv"][0], j + 1)
                nc.scalar.activation(cv[0][:, :], cv[0][:, :], ACT.Silu).then_inc(ff["silu"], 1)

            def z_hi_part(j, zi, f):
                e.wait_ge(ff["mul"], j + 1)
                if f is not None:
                    e.wait_ge(used[D1], n_split(ph, D1, f))
                nc.scalar.copy(z_hi[zi][:, 0:TP], cv[1][:, 0:TP])
                nc.scalar.copy(z_hi[zi][:, TP:T].rearrange("p (n t) -> p n t", t=TS_), cv_sam(cv[1])).then_inc(ff["zh"], 1)

            def down(f):
                for m in range(KD):
                    need = (ff["dn"], 7 * f + m + 1) if m < 7 else (used[D1], n_split(ph, D1, f) + 1)
                    act_result(e, need, m % 2, tb[m % 2], mod[:, q_gate + m, 0:1], None, None, xb + 8 * f + m - 1)
                    if isinstance(f, int) and m >= 1:
                        after_last(m - 1)

            e.wait_ge(ff["load"], 16)
            e.wait_ge(ff["load2"], 16)
            e.wait_ge(ff["zero"], 1)
            ups(0, jb, True)
            z_hi_part(0, 0, None)
            ups(1, jb + 1)
            z_hi_part(1, 1, None)
            with e.Fori(1, NG) as f:
                ups(2 * f, 6 * f - 4 + jb)
                down(f - 1)
                z_hi_part(2 * f, 0, f)
                ups(2 * f + 1, 6 * f + 1 + jb)
                z_hi_part(2 * f + 1, 1, f)
            down(NG - 1)
            after_last(KD - 1)

        def act_branch(dst, c, g, scale):
            for b in range(NC):
                w = CW if b < 2 else TP - 2 * CW
                nc.scalar.activation(branch_view(dst, g, b * CW, b * CW + w), as_residues(bank[3 * (c % 2) + b][:, 0:w], g),
                                     ACT.Identity, scale=scale)
            nc.scalar.activation(dst[:, TP:T], bank[3 * (c % 2) + 2][:, TP - 2 * CW:CW], ACT.Identity, scale=scale
                                 ).then_inc(job_free[c % 2], 1)

        def act_attention(e):
            e.wait_ge(at_["smax"], 1)
            nc.scalar.activation(lsam[:, :, :], lsam[:, :, :], ACT.Exp, bias=cols[:, 1, 0:1], accum_out=cols[:, 2, 0:1]
                                 ).then_inc(at_["sexp"], 1)

            def exps(i):
                g = (i % 6) // 2
                e.wait_ge(at_["nm"], i + 1)
                for b in range(8):
                    lo = 0 if PREV[g][b] else P
                    last = nc.scalar.activation(lg[i % 2][:, b, lo:256], lg[i % 2][:, b, lo:256], ACT.Exp,
                                                bias=stat[:, 1, i, b:b + 1], accum_out=stat[:, 2, i, b:b + 1])
                last.then_inc(at_["exp"], 1)

            exps(0)
            for i in range(12):
                g, j = (i % 6) // 2, i // 6
                if i < 11:
                    exps(i + 1)
                for q in range(4):
                    n = 4 * i + q
                    e.wait_ge(at_["t_done"], n + 1)
                    if n >= 2:
                        e.wait_ge(at_["pv"], n - 1)
                    if g < 2:
                        lo = 0 if PREV[g][2 * q] else P
                        nc.scalar.copy(pt[n % 2][:, lo:512], bank[2 + n % 2][:, lo:512]).then_inc(at_["pt"], 1)
                    else:
                        nc.scalar.copy(pt[n % 2][:, :].rearrange("p (b k) -> p b k", b=2)[:, :, P:256],
                                       bank[2 + n % 2][:, :].rearrange("p (b k) -> p b k", b=2)[:, :, P:256]
                                       ).then_inc(at_["pt"], 1)
                if i % 6 == 5:
                    e.wait_ge(at_["exp"], i + 1)
                    nc.scalar.activation(stat[:, 2, 6 * j:6 * j + 6, :], stat[:, 2, 6 * j:6 * j + 6, :], ACT.Ln
                                         ).then_inc(at_["ln"], 1)
                    for n in range(6 * j, 6 * j + 6):
                        gg, hb = (n % 6) // 2, n % 2
                        e.wait_ge(at_["lb"], n + 1)
                        if n >= 6:
                            e.wait_ge(at_["o_ready"], 3)
                        d = DIL[gg]
                        if d == 1:
                            nc.scalar.copy(lse[gg][:, 512 * hb:512 * hb + 512], bank[6][:, :]).then_inc(at_["ls"], 1)
                        else:
                            nc.scalar.copy(as_residues(lse[gg][:, :], gg)[:, d // 2 * hb:d // 2 * (hb + 1), :],
                                           bank[6][:, :].rearrange("p (r i) -> p r i", r=d // 2)).then_inc(at_["ls"], 1)
                    for gg in range(3):
                        e.wait_ge(at_["sub"], 3 * j + gg + 1)
                        nc.scalar.activation(lse[gg][:, :], lse[gg][:, :], ACT.Exp).then_inc(at_["e"], 1)
                    for gg in range(3):
                        e.wait_ge(at_["z"], 3 * j + gg + 1)
                        nc.scalar.copy(o_hi[:, 2 * gg + j, 0:TP], orow[gg][:, :]).then_inc(at_["hi"], 1)

        @block.scalar
        def _(e):
            e.wait_ge(params[0], 16)
            nc.scalar.activation(cact[:, :, :], cact[:, :, :], ACT.Silu).then_inc(c_sem, 1)
            e.wait_ge(c_sem, 1)
            nc.scalar.copy(c_spl[:, :, 0:10], cact[:, :, :]).then_inc(c_sem, 1)
            e.wait_ge(params[1], 16)
            for i in range(4):
                for s in range(4):
                    put_hi(e, "mod", s, i, first=(i == 0), act=True)
                for s in range(4):
                    take_mod(e, "mod", s, i, s % 2, 4 * i + s)
                for k in (2 * i, 2 * i + 1):
                    act_square(e, 0, k, x, sq, (xload[k // 4], 16))
            act_root(e, 0)
            act_wide(e, 0, rstd)
            act_ada(e, 0, Q_SHM0, tmp, 0)
            def w1_act(i):
                for mm in range(2):
                    m = 2 * i + mm
                    e.wait_ge(used[A0], n_split("w1", A0, m) + 1)
                    if not (isinstance(m, int) and m == 0):
                        e.wait_ge(job_free[1], m)
                    for c in range(NC):
                        last = nc.scalar.activation(sg[:, c * CW:(c + 1) * CW], bank[c][:, 0:CW], ACT.Sigmoid,
                                                    bias=col(P_B1G, m))
                    last.then_inc(job_free[0], 1)
                    for j in range(12):
                        if j < 10:
                            put_hi(e, "w1", D0 + j % 2, 6 * m + j // 2 + 1, act=True)
                        take_mod(e, "w1", D0 + j % 2, 6 * m + j // 2, j % 2, 16 + 12 * m + j)

            w1_act(0)
            with e.Fori(1, 4) as i:
                w1_act(i)
            for b in range(2):
                e.wait_ge(cap_out[b], 128)
            act_wide(e, 1, mu)
            for k in range(KD):
                act_square(e, 1, k, ycv, tb, (centred, k + 1))
            act_root(e, 1)
            act_wide(e, 2, rstd)
            for k in range(KD):
                e.wait_ge(h_pre, 8 + k + 1)
                if k >= 2:
                    e.wait_ge(h_ready, 8 + k - 1)
                nc.scalar.activation((mu, ysq)[k % 2][:, :], ycv[:, k, :], ACT.Silu, scale=col(P_LNG, k),
                                     bias=col(P_LNB, k)).then_inc(h_aff, 1)
                e.wait_ge(h_aff, 8 + k + 1)
                nc.scalar.copy(h_hi[:, k, :], (mu, ysq)[k % 2][:, :]).then_inc(h_hi_done, 1)
            for m in range(KD):
                s = m % 4
                act_result(e, (used[s], n_split("w2", s, m // 4) + 1), m % 2, tb[m % 2], mod[:, Q_GM0 + m, 0:1],
                           b2g[:, m:m + 1], col(P_B2, m), m - 1 if m >= 2 else None)
                if m >= 1:
                    act_square(e, 2, m - 1, x, sq, (x_final, m))
            act_square(e, 2, 7, x, sq, (x_final, 8))
            act_root(e, 2)
            act_wide(e, 3, rstd)
            act_ada(e, 2, Q_SHF0, tmp, 2)
            act_ffn(e, 0, Q_GF0, lambda m: act_square(e, 3, m, x, sq, (x_final, 88 + m + 1)))
            act_root(e, 3)
            act_wide(e, 4, rstd)
            act_ada(e, 3, Q_SHKV, tmp, 3)
            for c in range(6):
                g = c // 2
                e.wait_ge(used[c % 2], n_split("kv", c % 2, c // 2) + 1)
                if c >= 2:
                    e.wait_ge(kst_out[c % 2], 16 * (c // 2))
                act_branch(kst[c % 2], c, g, 1.0)
            for s in (D0, D1):
                e.wait_ge(used[s], n_split("kv", s, 2) + 1)
            act_ada(e, 4, Q_SHM1, tmp, 4)
            for b in range(2):
                e.wait_ge(kst_out[b], 48)
            for c in range(6):
                e.wait_ge(used[c % 2], n_split("q", c % 2, c // 2) + 1)
                act_branch(qt[:, c, :], c, c // 2, 0.125)
            act_attention(e)
            for m in range(KD):
                s = m % 4
                act_result(e, (used[s], n_split("wo", s, m // 4) + 1), m % 2, tb[m % 2], mod[:, Q_GM1 + m, 0:1],
                           None, None, XB["wo"] + m - 1 if m >= 2 else None)
                if m >= 1:
                    act_square(e, 4, m - 1, x, sq, (x_final, XB["wo"] + m))
            act_square(e, 4, 7, x, sq, (x_final, XB["wo"] + 8))
            act_root(e, 4)
            act_wide(e, 5, rstd)
            act_ada(e, 5, Q_SHF1, tmp, 5)
            act_ffn(e, 1, Q_GF1, lambda m: act_square(e, 5, m, x, sq, (x_final, XB["ffn1"] + 80 + m + 1)))
            act_root(e, 5)
            act_wide(e, 6, rstd)

        def dve_ffn(e, l, q_gate, r):
            ph, ff, jb, xb = f"ffn{l}", FF[l], JB[f"ffn{l}"], XB[f"ffn{l}"]

            def convs(j, ch):
                cb = j if isinstance(j, int) else None
                for w in range(2):
                    c0 = j + NJ * w
                    cs = slice(c0, c0 + 1) if cb is not None else bass.ds(c0, 1)
                    e.wait_ge(ff["op1"][w], j + 1)
                    ch(e.scalar_tensor_tensor(cv[w][:, :], u[w][:, 1:1 + UC], cwb[:, cs, 1:2].rearrange("p o n -> p (o n)"),
                                              cv[w][:, :], ALU.mult, ALU.add))
                    e.scalar_tensor_tensor(cv[w][:, :], u[w][:, 2:2 + UC], cwb[:, cs, 2:3].rearrange("p o n -> p (o n)"),
                                           cv[w][:, :], ALU.mult, ALU.add).then_inc(ff["conv"][w], 1)
                e.wait_ge(ff["silu"], j + 1)
                e.wait_ge(ff["conv"][1], j + 1)
                e.tensor_tensor(cv[1][:, :], cv[0][:, :], cv[1][:, :], ALU.mult).then_inc(ff["mul"], 1)

            def down(f, ch, last=False):
                for m in range(KD):
                    dve_result(e, ch, (job_free[m % 2], 6 * f + jb + 4 + m // 2 - (1 if last else 0)), tb[m % 2],
                               mod[:, q_gate + m, 1:9], x[:, m, :])
                    if last and m >= 1:
                        dve_add_square(e, r, m - 1, sq, acc)

            e.memset(u[0][:, 0:2], 0.0)
            e.memset(u[1][:, 0:2], 0.0).then_inc(ff["zero"], 1)
            ch = Chain(e, ff["dve"])
            convs(0, ch)
            convs(1, ch)
            assert ch.n == 4
            with e.Fori(1, NG) as f:
                ch = Chain(e, ff["dve"], 12 * f - 8)
                convs(2 * f, ch)
                down(f - 1, ch)
                convs(2 * f + 1, ch)
            ch = Chain(e, ff["dve"], 12 * NG - 8)
            down(NG - 1, ch, last=True)
            dve_add_square(e, r, KD - 1, sq, acc)

        def dve_attention(e):
            ch = Chain(e, at_["chain"])
            for b in range(2):
                e.wait_ge(job_free[b], JB["q"] + 3)
            ch(e.memset(qd[:, :, :, :], 0.0))
            e.tensor_copy(qd[0:64, :, :, 0], qt[0:64, :, TP:T])
            e.tensor_copy(qd[64:P, :, :, 1], qt[64:P, :, TP:T]).then_inc(at_["qd"], 1)
            e.wait_ge(at_["sc"], 1)
            e.tensor_copy(s_sb[:, :], bank[0][:, 0:384])
            e.tensor_copy(sn_sb[:, :], bank[1][0:TSAM, 0:384]).then_inc(at_["ss"], 1)
            e.wait_ge(at_["st"], 1)
            e.wait_ge(att_in[3], 16)
            for g in range(3):
                last = e.tensor_tensor_reduce(lsam[:, g, :], bank[2][:, 160 * g:160 * g + 160], bsam[:, g, :], 1.0, NEG,
                                              ALU.add, ALU.max, cols[:, 0, g:g + 1])
            ch(last)
            ch(e.tensor_reduce(cols[:, 0, 3:4], cols[:, 0, 0:3], AX, ALU.max))
            e.tensor_scalar(cols[:, 1, 0:1], cols[:, 0, 3:4], -1.0, None, ALU.mult).then_inc(at_["smax"], 1)
            e.wait_ge(at_["sexp"], 1)
            ch(e.reciprocal(cols[:, 3, 0:1], cols[:, 2, 0:1]))
            e.tensor_scalar(lsam[:, :, :], lsam[:, :, :], cols[:, 3, 0:1], None, ALU.mult).then_inc(at_["sp"], 1)
            e.wait_ge(at_["sb"], 1)
            e.tensor_copy(pc[:, :], bank[3][:, 0:384])
            e.tensor_copy(pn[:, :], bank[0][0:TSAM, 0:384]).then_inc(at_["spc"], 1)

            def logits(i):
                g, hp, bt = (i % 6) // 2, i % 2, i // 2
                if hp == 0:
                    e.wait_ge(b_in[bt % 4], 16 * (bt // 4) + 16)
                if i >= 2:
                    e.wait_ge(at_["t_done"], 4 * i - 4)
                for q in range(4):
                    e.wait_ge(at_["s_done"], 4 * i + q + 1)
                    for b in (2 * q, 2 * q + 1):
                        lo = 0 if PREV[g][b] else P
                        last = e.tensor_tensor_reduce(
                            lg[i % 2][:, b, lo:256], bank[q % 2][:, (b % 2) * 256 + lo:(b % 2) * 256 + 256],
                            btab[:, bt % 4, hp, lo:256], 1.0, NEG, ALU.add, ALU.max, stat[:, 0, i, b:b + 1])
                    last.then_inc(at_["s_free"], 1)
                e.wait_ge(at_["s_free"], 4 * i + 4)
                e.tensor_scalar(stat[:, 1, i, :], stat[:, 0, i, :], -1.0, None, ALU.mult).then_inc(at_["nm"], 1)

            logits(0)
            for i in range(12):
                g, hp, j = (i % 6) // 2, i % 2, i // 6
                if i < 11:
                    logits(i + 1)
                e.wait_ge(at_["exp"], i + 1)
                ch(e.reciprocal(rsum[:, i, :], stat[:, 2, i, :]))
                for b in range(8):
                    lo = 0 if PREV[g][b] else P
                    e.tensor_scalar(lg[i % 2][:, b, lo:256], lg[i % 2][:, b, lo:256], rsum[:, i, b:b + 1], None,
                                    ALU.mult).then_inc(at_["p"], 1)
                if hp == 1:
                    e.wait_ge(at_["pv"], 4 * i + 4)
                    if j == 1:
                        e.wait_ge(at_["hi"], 3)
                    d = DIL[g]
                    for hb in range(2):
                        src = bank[4 + hb][:, :]
                        if d == 1:
                            last = e.tensor_copy(orow[g][:, 512 * hb:512 * hb + 512], src)
                        else:
                            last = e.tensor_copy(as_residues(orow[g][:, :], g)[:, d // 2 * hb:d // 2 * (hb + 1), :],
                                                 src.rearrange("p (r i) -> p r i", r=d // 2))
                    last.then_inc(at_["o_free"], 1)
                if i % 6 == 5:
                    e.wait_ge(at_["ln"], j + 1)
                    e.tensor_tensor(stat[:, 2, 6 * j:6 * j + 6, :], stat[:, 2, 6 * j:6 * j + 6, :],
                                    stat[:, 0, 6 * j:6 * j + 6, :], ALU.add).then_inc(at_["lse"], 1)
                    e.wait_ge(at_["ls"], 6 * j + 6)
                    ch(e.tensor_tensor(top[:, :], lse[0][:, :], lse[1][:, :], ALU.max))
                    ch(e.tensor_tensor(top[:, :], top[:, :], lse[2][:, :], ALU.max))
                    for gg in range(3):
                        e.tensor_tensor(lse[gg][:, :], lse[gg][:, :], top[:, :], ALU.subtract).then_inc(at_["sub"], 1)
                    e.wait_ge(at_["e"], 3 * j + 2)
                    ch(e.tensor_tensor(rz[:, :], lse[0][:, :], lse[1][:, :], ALU.add))
                    e.wait_ge(at_["e"], 3 * j + 3)
                    ch(e.tensor_tensor(rz[:, :], rz[:, :], lse[2][:, :], ALU.add))
                    ch(e.reciprocal(rz[:, :], rz[:, :]))
                    for gg in range(3):
                        ch(e.tensor_tensor(lse[gg][:, :], lse[gg][:, :], rz[:, :], ALU.mult))
                    e.wait_ge(at_["o_free"], 3 * j + 3)
                    for gg in range(3):
                        e.tensor_tensor(orow[gg][:, :], orow[gg][:, :], lse[gg][:, :], ALU.mult).then_inc(at_["z"], 1)
                    for gg in range(3):
                        e.wait_ge(at_["hi"], 3 * j + gg + 1)
                        e.tensor_tensor(o_lo[:, 2 * gg + j, 0:TP], orow[gg][:, :], o_hi[:, 2 * gg + j, 0:TP].bitcast(F),
                                        ALU.subtract).then_inc(at_["o_ready"], 1)
            e.wait_ge(at_["osam"], 1)
            ov = bank[7][:, 0:384].rearrange("p (c t h) -> p c t h", c=6, h=2)
            e.tensor_copy(osam[0:64, :, :], ov[0:64, :, :, 0])
            ch(e.tensor_copy(osam[64:P, :, :], ov[64:P, :, :, 1]))
            e.tensor_copy(o_hi[:, :, TP:T], osam[:, :, :]).then_inc(at_["o_ready"], 1)
            e.wait_ge(at_["o_ready"], 7)
            e.tensor_tensor(o_lo[:, :, TP:T], osam[:, :, :], o_hi[:, :, TP:T].bitcast(F), ALU.subtract
                            ).then_inc(at_["o_ready"], 1)

        @block.vector
        def _(e):
            ch = Chain(e, dve)
            e.memset(ones[:, :], 1.0).then_inc(consts, 1)
            for b in range(2):
                e.memset(full[b][:, 0:HA], 0.0)
            e.wait_ge(c_sem, 2)
            e.tensor_tensor(c_spl[:, :, 10:20], cact[:, :, :], c_spl[:, :, 0:10].bitcast(F), ALU.subtract).then_inc(c_lo, 1)
            for k in range(KD):
                dve_add_square(e, 0, k, sq, tb[1])
            dve_inverse_root(e, ch, 0, 0, EPS)
            for b in range(2):
                e.wait_ge(mod_free[b], 8)
            e.wait_ge(params[1], 16)
            dve_gain(e, ch, P_NM0, Q_SCM0)
            e.wait_ge(wide_sb, 1)
            dve_ada(e, ch, 0, Q_SHM0, tmp)
            ch(e.memset(ysum[:, :], 0.0))

            e.wait_ge(zero_out, 64)
            per = CA + 7
            n0 = ch.n
            with e.Fori(0, 4) as i:
                ch = Chain(e, dve, i * (2 * per) + n0)
                for b in range(2):
                    m = 2 * i + b
                    fb = full[b]
                    e.wait_ge(hist_in[b], 16 * i + 16)
                    e.wait_ge(job_free[0], m + 1)
                    e.wait_ge(used[A1], n_split("w1", A1, m) + 1)
                    b1 = col(P_B1A, m)
                    for c in range(NC):
                        w = CW if c < 2 else TP - 2 * CW
                        e.scalar_tensor_tensor(fb[:, HA + c * CW:HA + c * CW + w], bank[3 + c][:, 0:w], b1,
                                               sg[:, c * CW:c * CW + w], ALU.add, ALU.mult)
                    rows = fb[:, FS:FL].rearrange("p (n r) -> p n r", r=FSEG)
                    e.scalar_tensor_tensor(rows[:, :, HA:FSEG],
                                           bank[5][:, TP - 2 * CW:CW].rearrange("p (n t) -> p n t", t=TS_), b1,
                                           sg[:, TP:T].rearrange("p (n t) -> p n t", t=TS_), ALU.add, ALU.mult
                                           ).then_inc(job_free[1], 1)
                    e.wait_ge(job_free[1], m + 1)
                    y = ycv[:, bass.ds(m, 1), :].rearrange("p o n -> p (o n)")
                    taps = prm[:, bass.ds(m * CA + P_DW, CA)].unsqueeze(1).to_broadcast([P, NS, CA])
                    ysam = y[:, TP:T].rearrange("p (n t) -> p n t", t=TS_)
                    e.tensor_scalar(y[:, 0:TP], fb[:, 0:TP], prm[:, bass.ds(m * CA + P_DW, 1)], col(P_DWB, m),
                                    ALU.mult, ALU.add)
                    for t in range(TS_):
                        ch(e.tensor_tensor(scr, rows[:, :, t:t + CA], taps, ALU.mult))
                        ch(e.tensor_reduce(ysam[:, :, t:t + 1], scr, AX, ALU.add))
                    ch(e.tensor_scalar(y[:, TP:T], y[:, TP:T], col(P_DWB, m), None, ALU.add))
                    for w in range(1, CA):
                        ins_ = e.scalar_tensor_tensor(y[:, 0:TP], fb[:, w:w + TP],
                                                      prm[:, bass.ds(m * CA + P_DW + w, 1)], y[:, 0:TP], ALU.mult, ALU.add)
                        if w < CA - 1:
                            ch(ins_)
                    ins_.then_inc(conv_y, 1)
                    e.wait_ge(conv_y, m + 1)
                    e.tensor_tensor(ysum[:, :], ysum[:, :], y, ALU.add).then_inc(conv_done, 1)
                    e.wait_ge(conv_done, m + 1)
            ch = Chain(e, ln_dve)
            e.wait_ge(col_sum, 2)
            e.tensor_scalar(cols[:, 0, :], bank[6][:, 0:9], 1.0 / D, None, ALU.mult).then_inc(mean_col, 1)
            for b in range(2):
                e.wait_ge(mod_free[b], 56)
            ch(e.tensor_tensor(b2g[:, :], prm[:, P_B2:P_B2 + 8], mod[:, Q_GM0:Q_GM0 + 8, 0:1].rearrange("p k o -> p (k o)"),
                               ALU.mult))
            dve_gain(e, ch, P_NF0, Q_SCF0)
            e.wait_ge(wide_sb, 2)
            for k in range(KD):
                e.tensor_tensor(ycv[:, k, :], ycv[:, k, :], mu[:, :], ALU.subtract).then_inc(centred, 1)
                if k >= 1:
                    dve_add_square(e, 1, k - 1, tb, ysq)
            dve_add_square(e, 1, 7, tb, ysq)
            dve_inverse_root(e, ch, 1, 2, LN_EPS)
            e.wait_ge(wide_sb, 3)
            for k in range(KD):
                e.wait_ge(centred, 8)
                e.tensor_tensor(ycv[:, k, :], ycv[:, k, :], rstd[:, :], ALU.mult).then_inc(h_pre, 1)
            for m in range(KD):
                dve_result(e, ch, (job_free[m % 2], 8 + m // 2 + 1), tb[m % 2], mod[:, Q_GM0 + m, 1:9], x[:, m, :])
                if m >= 1:
                    dve_add_square(e, 2, m - 1, sq, acc)
            dve_add_square(e, 2, 7, sq, acc)
            dve_inverse_root(e, ch, 2, 3, EPS)
            e.wait_ge(wide_sb, 4)
            dve_ada(e, ch, 2, Q_SHF0, tmp)
            dve_ffn(e, 0, Q_GF0, 3)
            dve_inverse_root(e, ch, 3, 4, EPS)
            dve_gain(e, ch, P_NKV, Q_SCKV)
            e.wait_ge(wide_sb, 5)
            dve_ada(e, ch, 3, Q_SHKV, tmp)
            e.wait_ge(h_hi_done, 32)
            dve_gain(e, ch, P_NM1, Q_SCM1)
            e.wait_ge(cfo_out[0], 16)
            for n in range(27):
                g, t = n // 9, n % 9
                if t < 8:
                    e.wait_ge(v_done, 8 * g + t + 1)
                else:
                    e.wait_ge(used[D1], n_split("kv", D1, g) + 1)
                if n >= 4:
                    e.wait_ge(vst_out[n % 4], 16 * (n // 4))
                r0 = 0 if t < 8 else P - TSAM
                e.tensor_copy(vst[n % 4][r0:P, :], bank[6 + n % 2][r0:P, 0:256]).then_inc(v_free[n % 2], 1)
            dve_ada(e, ch, 4, Q_SHM1, tmp)
            e.wait_ge(h_hi_done, 40)
            dve_gain(e, ch, P_NF1, Q_SCF1)
            dve_attention(e)
            for m in range(KD):
                dve_result(e, ch, (job_free[m % 2], JB["wo"] + m // 2 + 1), tb[m % 2], mod[:, Q_GM1 + m, 1:9], x[:, m, :])
                if m >= 1:
                    dve_add_square(e, 4, m - 1, sq, acc)
            dve_add_square(e, 4, 7, sq, acc)
            dve_inverse_root(e, ch, 4, 5, EPS)
            e.wait_ge(wide_sb, 6)
            dve_ada(e, ch, 5, Q_SHF1, tmp)
            dve_ffn(e, 1, Q_GF1, 5)
            dve_inverse_root(e, ch, 5, 6, EPS)
            e.wait_ge(wide_sb, 7)
            for k in range(KD):
                e.scalar_tensor_tensor(x[:, k, :], x[:, k, :], col(P_NFIN, k), rstd[:, :], ALU.mult, ALU.mult
                                       ).then_inc(y_ready, 1)

        def pe_ffn(e, l, a):
            ph, ff, jb = f"ffn{l}", FF[l], JB[f"ffn{l}"]

            def ups(j, job):
                for w in range(2):
                    product(e, ph, A0 + w, j, w, job, h_hi, h_lo, ready=(h_ready, 8 * a))

            def down(f, job):
                e.wait_ge(split[D0], n_split(ph, D0, f) + 1)
                e.wait_ge(split[D1], n_split(ph, D1, f) + 1)
                e.wait_ge(ff["zl"], 2 * f + 2)
                for m in range(KD):
                    b = m % 2
                    e.wait_ge(job_free[b], job + m // 2)
                    for zi in range(2):
                        s = D0 + zi
                        for q, (w, z) in enumerate(((w_hi, z_hi), (w_hi, z_lo), (w_lo, z_hi))):
                            for c in range(NC):
                                mm = e.matmul(bank[3 * b + c][:, 0:CW], w[s][:, m * P:(m + 1) * P],
                                              z[zi][:, c * CW:(c + 1) * CW], start=(zi == 0 and q == 0),
                                              stop=(zi == 1 and q == 2))
                        if m == KD - 1:
                            mm.then_inc(used[s], 1)
                    if m < KD - 1:
                        mm.then_inc(ff["dn"], 1)

            ups(0, jb)
            ups(1, jb + 1)
            with e.Fori(1, NG) as f:
                ups(2 * f, 6 * f + (jb - 4))
                down(f - 1, 6 * f + (jb - 3))
                ups(2 * f + 1, 6 * f + (jb + 1))
            down(NG - 1, 6 * NG - 4 + jb)

        def pe_attention(e):
            e.wait_ge(at_["qd"], 1)
            for n in range(18):
                s, k = n % 4, n // 4
                e.wait_ge(landed[s], 16 * (n_land("att", s, k) + 1))
                for pr in range(2):
                    if n < 16:
                        g, q0 = 1 + n // 8, TS_ * (n % 8)
                        for t in range(TS_):
                            cc = ((2 * g + pr) * TSAM + q0 + t) * 2
                            mm = e.matmul(bank[0][:, cc:cc + 2], w_raw[s][:, (pr * TS_ + t) * P:(pr * TS_ + t + 1) * P],
                                          qd[:, 2 * g + pr, q0 + t, :], start=True, stop=True)
                    else:
                        for nn in range(4):
                            q0 = TS_ * (4 * (n - 16) + nn)
                            cc = (pr * TSAM + q0) * 2
                            mm = e.matmul(bank[0][:, cc:cc + 8], w_raw[s][:, (nn * 2 + pr) * P:(nn * 2 + pr + 1) * P],
                                          qd[:, pr, q0:q0 + TS_, :].rearrange("p t h -> p (t h)"), start=True, stop=True)
                mm.then_inc(att_used[s], 1)
            e.wait_ge(att_in[0], 16)
            for c in range(6):
                mm = e.matmul(bank[1][0:TSAM, 64 * c:64 * c + 64], kt[:, c, TP:T], qd[:, c, :, :].rearrange("p t h -> p (t h)"),
                              start=True, stop=True)
            mm.then_inc(at_["sc"], 1)
            e.wait_ge(at_["ss"], 1)
            for g in range(3):
                e.transpose(bank[2][:, 160 * g:160 * g + P], s_sb[:, P * g:P * g + P], ident[:, :])
                mm = e.transpose(bank[2][:, 160 * g + P:160 * g + 160], sn_sb[:, P * g:P * g + P], ident[0:TSAM, 0:TSAM])
            mm.then_inc(at_["st"], 1)
            e.wait_ge(at_["sp"], 1)
            for g in range(3):
                e.transpose(bank[3][:, P * g:P * g + P], lsam[:, g, 0:P], ident[:, :])
                mm = e.transpose(bank[0][0:TSAM, P * g:P * g + P], lsam[:, g, P:160], ident[:, :])
            mm.then_inc(at_["sb"], 1)
            e.wait_ge(at_["spc"], 1)
            e.wait_ge(att_in[2], 16)
            for c in range(6):
                e.matmul(bank[7][:, 64 * c:64 * c + 64], vn[:, P * c:P * c + P], pn[:, 64 * c:64 * c + 64],
                         start=(c == 0), stop=False, skip_group_check=True)

            def scores(i):
                g, hp, j = (i % 6) // 2, i % 2, i // 6
                c, r = 2 * g + j, slice(64 * hp, 64 * hp + 64)
                for q in range(4):
                    n = 4 * i + q
                    if n >= 2:
                        e.wait_ge(at_["s_free"], n - 1)
                    for b in (2 * q, 2 * q + 1):
                        pv = PREV[g][b]
                        lo = 0 if pv else P
                        mm = e.matmul(bank[q % 2][:, (b % 2) * 256 + lo:(b % 2) * 256 + 256], qt[r, c, b * P:b * P + P],
                                      kt[r, c, (b - pv) * P:(b + 1) * P], start=True, stop=True)
                    mm.then_inc(at_["s_done"], 1)

            def turn(i, q):
                g = (i % 6) // 2
                n = 4 * i + q
                e.wait_ge(at_["p"], 8 * i + 2 * q + 2)
                if n >= 2:
                    e.wait_ge(at_["pt"], n - 1)
                for b in (2 * q, 2 * q + 1):
                    for half in ((0, 1) if PREV[g][b] else (1,)):
                        cc = ((b % 2) * 2 + half) * P
                        mm = e.transpose(bank[2 + n % 2][:, cc:cc + P], lg[i % 2][:, b, half * P:half * P + P], ident[:, :])
                mm.then_inc(at_["t_done"], 1)

            def values(i, q):
                g, hp, j = (i % 6) // 2, i % 2, i // 6
                n, h = 4 * i + q, 2 * j + hp
                e.wait_ge(at_["pt"], n + 1)
                if hp == 0 and q == 0 and i > 0:
                    e.wait_ge(at_["o_free"], i // 2)
                for b in (2 * q, 2 * q + 1):
                    halves = (0, 1) if PREV[g][b] else (1,)
                    for half in halves:
                        cc = ((b % 2) * 2 + half) * P
                        mm = e.matmul(bank[4 + b // 4][64 * hp:64 * hp + 64, (b % 4) * P:(b % 4 + 1) * P],
                                      v_sb[g][:, b - 1 + half, 64 * h:64 * h + 64], pt[n % 2][:, cc:cc + P],
                                      start=(half == halves[0]), stop=(half == 1))
                mm.then_inc(at_["pv"], 1)

            def sample_values(n):
                s, k = n % 4, n // 4
                e.wait_ge(landed[s], 16 * (n_land("att", s, k) + 1))
                m = n - 18
                for pr in range(2):
                    if m < 16:
                        g, q0 = 1 + m // 8, TS_ * (m % 8)
                        for t in range(TS_):
                            cc = ((2 * g + pr) * TSAM + q0 + t) * 2
                            mm = e.matmul(bank[7][:, cc:cc + 2], w_raw[s][:, t * 256 + pr * P:t * 256 + pr * P + P],
                                          pc[:, cc:cc + 2], start=False, stop=(m == 17), skip_group_check=True)
                    else:
                        for nn in range(4):
                            cc = (pr * TSAM + TS_ * (4 * (m - 16) + nn)) * 2
                            mm = e.matmul(bank[7][:, cc:cc + 8], w_raw[s][:, nn * 256 + pr * P:nn * 256 + pr * P + P],
                                          pc[:, cc:cc + 8], start=False, stop=(m == 17), skip_group_check=True)
                mm.then_inc(att_used[s], 1)

            nv = 18
            scores(0)
            for i in range(12):
                g, j = (i % 6) // 2, i // 6
                if i < 11:
                    scores(i + 1)
                if i % 2 == 0 and j == 0:
                    for a in ((1,), (4,), (5, 6))[g]:
                        e.wait_ge(att_in[a], 16)
                turn(i, 0)
                for q in range(4):
                    if q < 3:
                        turn(i, q + 1)
                    values(i, q)
                for _ in range(2 if i < 6 else 1):
                    sample_values(nv)
                    nv += 1
                if i % 6 == 5:
                    e.wait_ge(at_["lse"], j + 1)
                    for n in range(6 * j, 6 * j + 6):
                        gg, hb = (n % 6) // 2, n % 2
                        if n:
                            e.wait_ge(at_["ls"], n)
                        for b in range(4):
                            bb = 4 * hb + b
                            for hp in range(2):
                                mm = e.matmul(bank[6][64 * hp:64 * hp + 64, b * P:b * P + P],
                                              stat[:, 2, 6 * j + 2 * gg + hp, bb:bb + 1].to_broadcast([P, 64]),
                                              ident[:, :], start=True, stop=True)
                        mm.then_inc(at_["lb"], 1)
            e.wait_ge(att_used[1], 9)
            e.nop().then_inc(at_["osam"], 1)

        @block.tensor
        def _(e):
            e.wait_ge(params[2], 16)
            e.wait_ge(consts, 1)
            e.wait_ge(c_lo, 1)
            for i in range(4):
                for s in range(4):
                    modulate(e, "mod", s, i, s % 2, 2 * i + s // 2, first=(i == 0 and s < 2))
            e.wait_ge(mod_free[0], 8)
            pe_sum(e, 0, tb[1], (sq_added, 8))
            pe_wide(e, 4, (col_inv, 1))

            def w1_pe(i):
                for mm in range(2):
                    m = 2 * i + mm
                    for s in (A0, A1):
                        product(e, "w1", s, m, s, m, h_hi, h_lo, ready=(h_ready, 0), first=isinstance(m, int) and m == 0)
                        for j in range(6 * s, 6 * s + 6):
                            modulate(e, "w1", D0 + j % 2, 6 * m + j // 2, j % 2, 6 * m + 8 + j // 2)

            w1_pe(0)
            with e.Fori(1, 4) as i:
                w1_pe(i)
            e.wait_ge(mod_free[0], 56)
            pe_sum(e, 1, ysum, (conv_done, 8))
            pe_wide(e, 0, (mean_col, 1))
            pe_sum(e, 2, ysq, (sq_added, 16))
            pe_wide(e, 4, (col_inv, 2))
            for m in range(KD):
                product(e, "w2", m % 4, m // 4, m % 2, 8 + m // 2, h_hi, h_lo, ready=(h_ready, 8))
            pe_sum(e, 3, acc, (sq_added, 24))
            pe_wide(e, 4, (col_inv, 3))
            pe_ffn(e, 0, 2)
            pe_sum(e, 4, acc, (sq_added, 32))
            pe_wide(e, 4, (col_inv, 4))
            for c in range(6):
                product(e, "kv", c % 2, c // 2, c % 2, JB["k"] + c // 2, h_hi, h_lo, ready=(h_ready, 24))
            for g in range(3):
                for s in (D0, D1):
                    e.wait_ge(split[s], n_split("kv", s, g) + 1)
                for t in range(9):
                    n = 9 * g + t
                    t0 = t * P if t < 8 else T - P
                    if n >= 2:
                        e.wait_ge(v_free[n % 2], n // 2)
                    for kk in range(KD):
                        s = D0 + kk // 4
                        c0 = (kk % 4) * 256
                        for q, (a, w) in enumerate(((h_hi, w_hi), (h_lo, w_hi), (h_hi, w_lo))):
                            mm = e.matmul(bank[6 + n % 2][:, 0:256], a[:, kk, t0:t0 + P], w[s][:, c0:c0 + 256],
                                          start=(kk == 0 and q == 0), stop=(kk == KD - 1 and q == 2))
                        if t == 8 and kk % 4 == 3:
                            mm.then_inc(used[s], 1)
                    if t < 8:
                        mm.then_inc(v_done, 1)
            for c in range(6):
                product(e, "q", c % 2, c // 2, c % 2, JB["q"] + c // 2, h_hi, h_lo, ready=(h_ready, 32))
            pe_attention(e)
            e.wait_ge(at_["o_ready"], 8)
            for m in range(KD):
                product(e, "wo", m % 4, m // 4, m % 2, JB["wo"] + m // 2, o_hi, o_lo, nk=6)
            pe_sum(e, 5, acc, (sq_added, 40))
            pe_wide(e, 4, (col_inv, 5))
            pe_ffn(e, 1, 5)
            pe_sum(e, 6, acc, (sq_added, 48))
            pe_wide(e, 4, (col_inv, 6))


def m_unit(w, m):
    k = w.shape[0] // P
    return w[:, m * P:(m + 1) * P].reshape(k, P, P).transpose(1, 0, 2).reshape(P, k * P)


def stream(i):
    units = []
    mods = [m_unit(i["w_mod"][0], q) for q in range(48)] + [m_unit(i["w_mod_kv"], q) for q in range(16)] + \
        [m_unit(i["w_mod"][1], q) for q in range(48)]
    units += mods[:16]
    for m in range(8):
        units += [m_unit(i["a_w1"][0], 8 + m), m_unit(i["a_w1"][0], m)]
        units += mods[16 + 12 * m:28 + 12 * m]
    units += [m_unit(i["a_w2"][0], m) for m in range(8)]

    def ffn(l):
        up = [[m_unit(i["f_wup"][l], j), m_unit(i["f_wup"][l], NJ + j)] for j in range(NJ)]
        dn = [i["f_wdown"][l][j * P:(j + 1) * P] for j in range(NJ)]
        out = up[0] + up[1]
        for f in range(1, NG):
            out += up[2 * f] + dn[2 * f - 2:2 * f] + up[2 * f + 1]
        return out + dn[NJ - 2:]

    units += ffn(0)
    for c in range(6):
        units.append(m_unit(i["w_kv"], c))
    for gg in range(3):
        v = i["w_kv"][:, 768 + 256 * gg:768 + 256 * gg + 256].reshape(2, 4, P, 256)
        units += [v[hf].transpose(1, 0, 2).reshape(P, UNIT) for hf in range(2)]
    units += [m_unit(i["w_q"][0], c) for c in range(6)]
    for m in range(8):
        units.append(np.concatenate([m_unit(i["w_o"][0], m), np.zeros((P, 256), np.float32)], axis=1))
    units += ffn(1)
    return np.stack(units)


def chunks(v):
    return v.reshape(-1, P).T


def buckets(dist):
    d = np.maximum(dist, 1).astype(np.float32)
    large = 16 + (np.log(d / np.float32(16)) / np.float32(np.log(128.0)) * np.float32(16)).astype(np.int32)
    return np.where(dist < 16, dist, np.minimum(large, 31))


def bias_places():
    q, k = np.arange(P)[:, None], np.arange(2 * P)[None, :]
    at_p = []
    for g, dil in enumerate(DIL):
        m = q + P - k
        ok = (m >= 0) & (m <= SPAN)
        if g == 2:
            ok = ok & (k >= P) & (q // 64 == (k - P) // 64)
        at_p.append(np.where(ok, buckets(np.where(ok, m, 0) * dil), 32))
    tok, key = np.arange(TSAM)[:, None], np.arange(P + TSAM)[None, :]
    n, t = tok // TS_, tok % TS_
    at_s = []
    for g, dil in enumerate(DIL):
        new = key >= P
        kn, kt = (key - P) // TS_, (key - P) % TS_
        if g == 0:
            m = np.where(new, t - kt, P + t - key)
            ok = (m >= 0) & (m <= SPAN) & (~new | (kn == n))
        else:
            m = np.where(new, 0, P - key)
            ok = ~new | ((kn == n) & (kt == t))
        at_s.append(np.where(ok, buckets(np.where(ok, m, 0) * dil), 32))
    return np.stack(at_p), at_s


def cache_units(caches):
    units = []
    for kv in range(2):
        for g in (1, 2):
            d = DIL[g]
            c = caches[g][:, :, kv].reshape(NS, P, d, 256)[:, :, 0:TS_]
            for n in range(NS):
                if kv == 0:
                    units.append(c[n].reshape(P, TS_, 2, P).transpose(3, 2, 1, 0).reshape(P, UNIT))
                else:
                    units.append(c[n].reshape(P, UNIT))
        c = caches[0][:, :, kv].reshape(NS, P, 256)
        for n4 in range(2):
            cc = c[4 * n4:4 * n4 + 4]
            if kv == 0:
                units.append(cc.reshape(4, P, 2, P).transpose(3, 0, 2, 1).reshape(P, UNIT))
            else:
                units.append(cc.transpose(1, 0, 2).reshape(P, UNIT))
    return np.stack(units)


def lay_out(i):
    i = {k: np.asarray(v) for k, v in i.items()}
    xa = np.concatenate([i["x_prompt"][0], i["x_sample"].reshape(TSAM, D)], axis=0)
    c = np.concatenate([i["c_prompt"], i["c_sample"], np.zeros((1, D), np.float32)], axis=0)
    prm = [chunks(i["b_mod"][0]), chunks(i["b_mod_kv"]), chunks(i["b_mod"][1]), chunks(i["norm_mix"][0]),
           chunks(i["norm_ffn"][0]), chunks(i["norm_kv"]), chunks(i["norm_mix"][1]), chunks(i["norm_ffn"][1]),
           chunks(i["norm_f"]), chunks(i["a_b1"][0]), chunks(i["a_dwb"][0]), chunks(i["a_ln_g"][0]),
           chunks(i["a_ln_b"][0]), chunks(i["a_b2"][0]),
           i["a_dw"][0].reshape(CA, KD, P).transpose(2, 1, 0).reshape(P, KD * CA)]
    cwb = np.stack([np.stack([*i["f_cw"][l].reshape(3, 2 * NJ, P), i["f_cb"][l].reshape(2 * NJ, P)]) for l in range(2)])
    rel = np.concatenate([i["rel_bias"], np.full((1, 12), NEG, np.float32)], axis=0)
    at_p, at_s = bias_places()
    bias_p = rel[at_p].transpose(3, 0, 1, 2)
    bias_p = np.stack([np.stack([bias_p[4 * g + 2 * j + hp, g] for hp in range(2)], axis=1)
                       for j in range(2) for g in range(3)])
    bias_s = np.stack([np.concatenate([
        np.stack([rel[at_s[g], 4 * g + 2 * j + hp] for hp in range(2)], axis=1).reshape(64, 160)
        for j in range(2)]) for g in range(3)], axis=1)
    caches = [i["cache_kv_w128"], i["cache_kv_w512"], i["cache_kv_w2048"]]
    d = {
        "bias_p": bias_p, "bias_s": bias_s, "att": cache_units(caches),
        "cache0": caches[0].reshape(NS, -1), "cache1": caches[1].reshape(NS, -1), "cache2": caches[2].reshape(NS, -1),
        "ws": stream(i),
        "xt": xa.reshape(T, KD, P).transpose(2, 1, 0),
        "ct": c.reshape(10, KD, P).transpose(2, 1, 0),
        "prm": np.concatenate(prm, axis=1),
        "cwb": cwb.transpose(0, 3, 2, 1),
        "hist_a": i["state_conv_a"][0].reshape(NS, HA, KD, P).transpose(2, 3, 0, 1).reshape(KD, P, NS * HA),
        "hist_f": i["state_conv_ffn"].reshape(2, NS, 2, 2 * NJ, P).transpose(0, 4, 3, 1, 2).reshape(2, P, 2 * NJ, 16),
        "ident": np.eye(P, dtype=np.float32),
    }
    return {k: np.ascontiguousarray(v) for k, v in d.items()}


OUTS = {"yt": (P, KD, T), "cap": (KD, P, 9 * HA), "cfo": (2, P, 2 * NJ, 18), "kt": (6, P, T), "v": (T, 768),
        "kvs0": (NS, (SPAN - TS_) * 512), "kvs1": (NS, (4 * SPAN - TS_) * 512), "kvs2": (NS, (16 * SPAN - TS_) * 512),
        "kvz": (4, P, UNIT)}


def assemble(o):
    y = o["yt"].transpose(2, 1, 0).reshape(T, D)
    keys = [o["kt"][2 * g:2 * g + 2].reshape(2, 2, 64, T) for g in range(3)]
    vals = [o["v"][:, 256 * g:256 * g + 256].reshape(T, 4, 64) for g in range(3)]
    prompt, sample = [], []
    for g, d in enumerate(DIL):
        k = keys[g]
        kp = k[..., :TP].reshape(2, 2, 64, d, TP // d).transpose(4, 3, 0, 1, 2).reshape(TP, 4, 64)
        kv = np.stack([kp, vals[g][:TP]], axis=1)
        w = SPAN * d
        if w <= TP:
            prompt.append(kv[TP - w:][None])
        else:
            pad = o["kvz"].reshape(w - TP, 2, 4, 64)
            prompt.append(np.concatenate([pad, kv], axis=0)[None])
        ks = k[..., TP:].transpose(3, 0, 1, 2).reshape(NS, TS_, 4, 64)
        new = np.stack([ks, vals[g][TP:].reshape(NS, TS_, 4, 64)], axis=2)
        sample.append(np.concatenate([o[f"kvs{g}"].reshape(NS, w - TS_, 2, 4, 64), new], axis=1))
    cap, cfo = o["cap"], o["cfo"]
    conv_a_p = cap[:, :, :HA].transpose(2, 0, 1).reshape(1, 1, HA, D)
    conv_a_s = cap[:, :, HA:].reshape(KD, P, NS, HA).transpose(2, 3, 0, 1).reshape(1, NS, HA, D)
    conv_f_p = cfo[..., :2].transpose(0, 3, 2, 1).reshape(2, 1, 2, 2 * DFF)
    conv_f_s = cfo[..., 2:].reshape(2, P, 2 * NJ, NS, 2).transpose(0, 3, 4, 2, 1).reshape(2, NS, 2, 2 * DFF)
    return (y[:TP][None], y[TP:].reshape(NS, TS_, D), *prompt, conv_a_p, conv_f_p, *sample, conv_a_s, conv_f_s)


def kernel(**inputs):
    import concourse.bacc as _bacc
    from concourse.bass_utils import run_bass_kernel_spmd as _run

    d = lay_out(inputs)
    nc = _bacc.Bacc("TRN2", target_bir_lowering=False, num_devices=1)
    ins = {k: nc.dram_tensor(f"in_{k}", a.shape, F, kind="ExternalInput").ap() for k, a in d.items()}
    outs = {k: nc.dram_tensor(f"out_{k}", s, F, kind="ExternalOutput").ap() for k, s in OUTS.items()}
    program(nc, ins, outs)
    r = _run(nc, [{f"in_{k}": a for k, a in d.items()}], core_ids=[0])
    return assemble({k: r.results[0][f"out_{k}"] for k in OUTS})
```

```python
from contextlib import ExitStack

import numpy as np
import concourse.bass as bass
from concourse import mybir

F = mybir.dt.float32
R = mybir.dt.float32r
ALU = mybir.AluOpType
ACT = mybir.ActivationFunctionType
AX = mybir.AxisListType.X

P = 128
D = 1024
KD = D // P
TP = 1024
NS, TS_ = 8, 4
TSAM = NS * TS_
T = TP + TSAM
NC = 3
CW = T // NC
DFF = 2816
NJ = DFF // P
NG = NJ // 2
CA = 31
HA = CA - 1
SPAN = 128
DIL = (1, 4, 16)
EPS, LN_EPS = 1e-6, 1e-5
NEG = -1e30

UNIT = 1024
A0, A1, D0, D1 = range(4)
UC = TP + 6 * NS
UL = UC + 6
FL = HA + TP + (HA + TS_) * NS
FS = HA + TP
FSEG = HA + TS_

NMOD = 112
P_BM = 0
P_NM0, P_NF0, P_NKV, P_NM1, P_NF1, P_NFIN = (NMOD + 8 * i for i in range(6))
P_B1A = P_NFIN + 8
P_B1G = P_B1A + 8
P_DWB, P_LNG, P_LNB, P_B2 = (P_B1G + 8 * (i + 1) for i in range(4))
P_DW = P_B2 + 8
P_END = P_DW + 8 * CA
Q_SHM0, Q_SCM0, Q_GM0, Q_SHF0, Q_SCF0, Q_GF0, Q_SHKV, Q_SCKV, Q_SHM1, Q_SCM1, Q_GM1, Q_SHF1, Q_SCF1, Q_GF1 = (
    8 * i for i in range(14))

PHASES = {}
LAND, SPLIT, FIRST = [0] * 4, [0] * 4, 0
for _name, _uses, _raw in (
        ("w1", (8, 8, 0, 0), 0), ("w2", (2, 2, 2, 2), 0),
        ("ffn0", (21, 21, 12, 12), 0), ("kv", (3, 3, 3, 3), 0), ("q", (2, 2, 1, 1), 0),
        ("att", (9, 9, 9, 9), 1), ("wo", (2, 2, 2, 2), 0), ("ffn1", (21, 21, 12, 12), 0)):
    PHASES[_name] = (FIRST, tuple(LAND), tuple(SPLIT))
    for _s in range(4):
        LAND[_s] += _uses[_s]
        SPLIT[_s] += 0 if _raw else _uses[_s]
    FIRST += 0 if _raw else sum(_uses)
N_ATT = 36


ARENA = 212800


def program(nc, ins, outs):
    with ExitStack() as ctx:
        enter = ctx.enter_context
        enter(nc.sbuf_tensor("arena", [P, ARENA // 4], F))
        start = nc.sbuf_base - ARENA

        def at(name, shape, dt, off):
            return nc.alloc_sbuf_tensor_at(name, shape, dt, offset=start + off, align_bytes=8)

        o = 0
        x = at("x", [P, KD, T], F, o); o += KD * T * 4
        o_h = o
        h_hi = at("h_hi", [P, KD, T], R, o_h)
        h_lo = at("h_lo", [P, KD, T], R, o_h + KD * T * 4)
        o += 2 * KD * T * 4
        o_split = o
        w_hi = [at(f"w_hi{s}", [P, UNIT], R, o + 8192 * s) for s in range(4)]
        w_lo = [at(f"w_lo{s}", [P, UNIT], R, o + 8192 * s + 4096) for s in range(4)]
        o += 4 * 8192
        w_raw = [at(f"w_raw{s}", [P, UNIT], F, o + 4096 * s) for s in range(4)]
        o += 4 * 4096
        w_mod = [at(f"w_mod{i}", [P, UNIT], F, o_split + 16384 + 4096 * i) for i in range(4)]
        mod_rows = [at(f"mod_rows{i}", [P, 512], F, o_split + 40960 + 2048 * i) for i in range(2)]
        o_f = o
        z_hi = [at(f"z_hi{i}", [P, T], R, o_f + 8448 * i) for i in range(2)]
        z_lo = [at(f"z_lo{i}", [P, T], R, o_f + 8448 * i + 4224) for i in range(2)]
        u = [at(f"u{i}", [P, UL], F, o_f + 16896 + UL * 4 * i) for i in range(2)]
        cv = [at(f"cv{i}", [P, UC], F, o_f + 16896 + UL * 8 + UC * 4 * i) for i in range(2)]
        ycv = at("ycv", [P, KD, T], F, o_f)
        tmp = [at(f"tmp{i}", [P, T], F, o_f + 4224 * i) for i in range(2)]
        kst = [at(f"kst{i}", [P, T], F, o_f + 8448 + 4224 * i) for i in range(2)]
        sq = [at(f"sq{i}", [P, T], F, o_f + 25600 + 4224 * i) for i in range(2)]
        o += 34112
        o_t = o
        tb = [at(f"tb{i}", [P, T], F, o_t + 4224 * i) for i in range(2)]
        rstd = at("rstd", [P, T], F, o_t)
        sg = at("sg", [P, T], F, o_t)
        ysum = at("ysum", [P, T], F, o_t + 4224)
        o += 8448
        o_m = o
        full = [at(f"full{i}", [P, FL], F, o_m + 5312 * i) for i in range(2)]
        mu = at("mu", [P, T], F, o_m)
        ysq = at("ysq", [P, T], F, o_m + 4224)
        hist = at("hist", [P, 2 * NJ, 16], F, o_m)
        ostate = at("ostate", [P, 2 * NJ, 18], F, o_m + 2816)
        cwb = at("cwb", [P, 2 * NJ, 4], F, o_m + 5984)
        acc = at("acc", [P, T], F, o_m + 6720)
        vst = [at(f"vst{i}", [P, 4, P], F, o_m + 2048 * i) for i in range(4)]
        o += 10960
        mod = at("mod", [P, NMOD, 9], F, o); o += NMOD * 9 * 4
        prm = at("prm", [P, P_END], F, o); o += P_END * 4
        o_c = o
        cact = at("cact", [P, KD, 10], F, o_c + 1024)
        o = o_c + 1408
        gain = at("gain", [P, KD, 9], F, o); o += 288
        b2g = at("b2g", [P, KD], F, o); o += 32
        ident = at("ident", [P, P], F, o); o += 512
        ones = at("ones", [P, 2], F, o); o += 32
        cols = at("cols", [P, 6, 9], F, o); o += 224
        tsam = at("tsam", [P, KD, TSAM], F, o_c)
        scr = tsam[:, :, :].rearrange("p k n -> p (k n)")[:, 0:NS * CA].rearrange("p (n w) -> p n w", w=CA)
        ysmp = at("ysmp", [P, NS, TS_], F, o); o += 128
        assert o <= ARENA, o

        kt = at("kt", [P, 6, T], F, o_h)
        v_sb = [at(f"v{g}", [P, 8, 256], F, o_h + 25344 + 8192 * g) for g in range(3)]
        lg = [at(f"logits{i}", [P, 8, 256], F, o_h + 49920 + 8192 * i) for i in range(2)]
        stat = at("stat", [P, 3, 12, 8], F, o_h + 66304)
        rsum = at("rsum", [P, 12, 8], F, o_c + 1024)
        qt = at("qt", [P, 6, T], F, o_f)
        btab = at("btab", [P, 4, 2, 256], F, o_f + 25344)
        o_hi = at("o_hi", [P, 6, T], R, o_h)
        o_lo = at("o_lo", [P, 6, T], R, o_f)
        lse = [at(f"lse{g}", [P, TP], F, o_split + 4096 * g) for g in range(3)]
        top = at("top", [P, TP], F, o_split + 12288)
        rz = at("rz", [P, TP], F, o_split + 16384)
        orow = [at(f"orow{g}", [P, TP], F, o_split + 20480 + 4096 * g) for g in range(3)]
        o_v = o_h + 25344
        mix = [(lse, top, rz), ([at(f"lse_b{g}", [P, TP], F, o_v + 4096 * g) for g in range(3)],
                                at("top_b", [P, TP], F, o_v + 12288), at("rz_b", [P, TP], F, o_v + 16384))]
        pt = [at(f"pt{i}", [P, 512], F, o_m + 2048 * i) for i in range(2)]
        s_sb = at("s_sb", [P, 384], F, o_m + 4096)
        sn_sb = at("sn_sb", [TSAM, 384], F, o_m + 5632)
        bsam = at("bsam", [P, 3, 160], F, o_m + 7168)
        lsam = at("lsam", [P, 3, 160], F, o_h + 49920 + 8192)
        qd = at("qd", [P, 6, TSAM, 2], F, o_t)
        vn = at("vn", [TSAM, 768], F, o_t + 1536)
        pc = at("pc", [P, 384], F, o_t + 4608)
        pn = at("pn", [TSAM, 384], F, o_t + 6144)
        osam = at("osam", [P, 6, TSAM], F, o_t + 7680)
        zeros = at("zeros", [P, UNIT], F, o_f + 16896)

        bank = [enter(nc.psum_tensor(f"bank{i}", [P, 512], F)) for i in range(8)]

        def sem(name):
            return enter(nc.semaphore(name))

        landed = [sem(f"landed{s}") for s in range(4)]
        hi_done = [sem(f"hi_done{s}") for s in range(4)]
        split = [sem(f"split{s}") for s in range(4)]
        used = [sem(f"used{s}") for s in range(4)]
        job_free = [sem(f"job_free{b}") for b in range(2)]
        mod_in = [sem(f"mod_in{s}") for s in range(4)]
        mod_used = [sem(f"mod_used{s}") for s in range(4)]
        rows_taken = sem("mod_rows_taken")
        turned = sem("mod_turned")
        mod_done = sem("mod_done")
        consts = sem("consts")
        params = [sem(f"params{i}") for i in range(3)]
        xload = [sem(f"xload{i}") for i in range(4)]

        def n_split(ph, s, k):
            return PHASES[ph][2][s] + k

        def n_land(ph, s, k):
            return PHASES[ph][1][s] + k

        def fetch(e, ph, s, n, k, first=False):
            if not first:
                e.wait_ge(split[s], n_split(ph, s, k))
            n = n + PHASES[ph][0]
            src = ins["ws"][n] if isinstance(n, int) else ins["ws"][bass.ds(n, 1)].rearrange("o p n -> p (o n)")
            e.dma_start(w_raw[s][:, :], src).then_inc(landed[s], 16)

        def pool_wait(e, s, n):
            e.wait_ge(s, n)
            if not isinstance(n, int):
                e.nop(nofuse=True)

        def put_hi(e, ph, s, k, first=False):
            if not first:
                e.wait_ge(used[s], n_split(ph, s, k))
            pool_wait(e, landed[s], 16 * n_land(ph, s, k) + 16)
            e.tensor_copy(w_hi[s][:, :], w_raw[s][:, :]).then_inc(hi_done[s], 1)

        def put_lo(e, ph, s, k):
            e.wait_ge(hi_done[s], n_split(ph, s, k) + 1)
            e.tensor_tensor(w_lo[s][:, :], w_raw[s][:, :], w_hi[s][:, :].bitcast(F), ALU.subtract).then_inc(split[s], 1)

        def put(e, ph, s, k, first=False):
            put_hi(e, ph, s, k, first)
            put_lo(e, ph, s, k)

        def product(e, ph, s, k, b, job, hi, lo, nk=KD):
            e.wait_ge(split[s], n_split(ph, s, k) + 1)
            e.wait_ge(job_free[b], job)
            for kk in range(nk):
                for q, (w, a) in enumerate(((w_hi, hi), (w_hi, lo), (w_lo, hi))):
                    for c in range(NC):
                        mm = e.matmul(bank[3 * b + c][:, 0:CW], w[s][:, kk * P:(kk + 1) * P],
                                      a[:, kk, c * CW:(c + 1) * CW], start=(kk == 0 and q == 0),
                                      stop=(kk == nk - 1 and q == 2))
            mm.then_inc(used[s], 1)

        def product_pair(e, ph, job, a_n, first=False):
            for s in (A0, A1):
                e.wait_ge(split[s], n_split(ph, s, 0) + 1)
                if not first:
                    e.wait_ge(job_free[s], job)
            for kk in range(KD):
                e.wait_ge(h_ready[kk % 2], 4 * a_n + kk // 2 + 1)
                for s in (A0, A1):
                    for q, (w, a) in enumerate(((w_hi, h_hi), (w_hi, h_lo), (w_lo, h_hi))):
                        for c in range(NC):
                            mm = e.matmul(bank[3 * s + c][:, 0:CW], w[s][:, kk * P:(kk + 1) * P],
                                          a[:, kk, c * CW:(c + 1) * CW], start=(kk == 0 and q == 0),
                                          stop=(kk == KD - 1 and q == 2))
                    if kk == KD - 1:
                        mm.then_inc(used[s], 1)

        def mod_fetch(e, g):
            for u in range(4):
                if not (isinstance(g, int) and g == 0):
                    e.wait_ge(mod_used[u], g)
                n = 4 * g + u
                src = ins["wm"][n] if isinstance(n, int) else ins["wm"][bass.ds(n, 1)].rearrange("o p n -> p (o n)")
                e.dma_start(w_mod[u][:, :], src).then_inc(mod_in[u], 16)

        def mod_group(e, g):
            if not (isinstance(g, int) and g == 0):
                e.wait_ge(rows_taken, g)
            for u in range(4):
                e.wait_ge(mod_in[u], 16 * g + 16)
                for half in range(2):
                    mm = e.matmul(bank[6][0:9, :], cact[:, 2 * u + half, 0:9], w_mod[u][:, 512 * half:512 * half + 512],
                                  start=(u == 0 and half == 0), stop=(u == 3 and half == 1))
                mm.then_inc(mod_used[u], 1)

        def mod_turn(e, g, par):
            e.wait_ge(rows_taken, g + 1)
            if not (isinstance(g, int) and g == 0):
                e.wait_ge(mod_done, g)
            for i in range(4):
                mm = e.matmul(bank[7][:, 9 * i:9 * i + 9], mod_rows[par][0:9, i * P:(i + 1) * P], ident[0:9, 0:9],
                              start=True, stop=True)
            mm.then_inc(turned, 1)

        def take_rows(e, g, par):
            e.wait_ge(mod_used[3], g + 1)
            if not (isinstance(g, int) and g < 2):
                e.wait_ge(turned, g - 1)
            nc.scalar.copy(mod_rows[par][0:9, :], bank[6][0:9, :]).then_inc(rows_taken, 1)

        def take_columns(e, g):
            e.wait_ge(turned, g + 1)
            for i in range(4):
                q = 4 * g + i
                qs = slice(q, q + 1) if isinstance(q, int) else bass.ds(q, 1)
                last = nc.scalar.activation(mod[:, qs, :].rearrange("p o n -> p (o n)"), bank[7][:, 9 * i:9 * i + 9],
                                            ACT.Identity, bias=prm[:, qs])
            last.then_inc(mod_done, 1)

        def col(base, m):
            return prm[:, base + m:base + m + 1] if isinstance(m, int) else prm[:, bass.ds(m + base, 1)]

        class Chain:

            def __init__(self, e, s, base=0):
                self.e, self.s, self.n = e, s, base

            def __call__(self, instruction):
                instruction.then_inc(self.s, 1)
                self.n = self.n + 1
                self.e.wait_ge(self.s, self.n)

        col_sum, col_val, col_root, col_inv, wide = (sem(f"norm_{x}") for x in ("sum", "val", "root", "inv", "wide"))
        wide_sb = sem("norm_wide_sb")
        sq_done, sq_added = sem("sq_done"), sem("sq_added")
        h_pre, h_aff, h_hi_done = (sem(f"h_{x}") for x in ("pre", "affine", "hi_done"))
        h_ready = [sem(f"h_ready_{x}") for x in ("even", "odd")]
        h_smp = sem("h_samples")
        pool_own, conv_smp = sem("pool_own"), sem("conv_samples")
        x_final = sem("x_final")
        ada_bufs = tmp + kst
        dve = sem("dve")

        def pe_sum(e, rs, src, need):
            e.wait_ge(*need)
            for t in range(9):
                lo = t * P if t < 8 else T - P
                mm = e.matmul(bank[6][:, t:t + 1], src[:, lo:lo + P], ones[:, 0:1], start=True, stop=True)
            mm.then_inc(col_sum, 1)

        def pe_wide(e, c, need):
            e.wait_ge(*need)
            for t in range(9):
                rhs = ident[:, :] if t < 8 else ident[:, P - TSAM:P]
                out = bank[t // 4][:, (t % 4) * P:(t % 4 + 1) * P] if t < 8 else bank[2][:, 0:TSAM]
                mm = e.matmul(out, cols[:, c, t:t + 1].to_broadcast([P, P]), rhs, start=True, stop=True)
            mm.then_inc(wide, 1)

        def act_wide(e, rs, dst):
            e.wait_ge(wide, rs + 1)
            for b, w in ((0, 512), (1, 512), (2, TSAM)):
                last = nc.scalar.copy(dst[:, 512 * b:512 * b + w], bank[b][:, 0:w])
            last.then_inc(wide_sb, 1)

        def act_root(e, r):
            e.wait_ge(col_val, r + 1)
            nc.scalar.activation(cols[:, 2, :], cols[:, 0, :], ACT.Sqrt).then_inc(col_root, 1)

        def dve_inverse_root(e, ch, r, rs, eps):
            e.wait_ge(col_sum, rs + 1)
            e.tensor_scalar(cols[:, 0, :], bank[6][:, 0:9], 1.0 / D, eps, ALU.mult, ALU.add).then_inc(col_val, 1)
            e.wait_ge(col_root, r + 1)
            ch(e.reciprocal(cols[:, 1, :], cols[:, 2, :]))
            ch(e.tensor_tensor(cols[:, 3, :], cols[:, 1, :], cols[:, 1, :], ALU.mult))
            ch(e.tensor_tensor(cols[:, 3, :], cols[:, 3, :], cols[:, 0, :], ALU.mult))
            ch(e.tensor_scalar(cols[:, 3, :], cols[:, 3, :], -0.5, 1.5, ALU.mult, ALU.add))
            e.tensor_tensor(cols[:, 4, :], cols[:, 1, :], cols[:, 3, :], ALU.mult).then_inc(col_inv, 1)

        def act_square(e, r, k, src, buf, need):
            e.wait_ge(*need)
            if k >= 2:
                e.wait_ge(sq_added, 8 * r + k - 1)
            nc.scalar.activation(buf[k % 2][:, :], src[:, k, :], ACT.Square).then_inc(sq_done, 1)

        def dve_add_square(e, r, k, buf, into):
            e.wait_ge(sq_done, 8 * r + k + 1)
            if k == 0:
                e.tensor_copy(into[:, :], buf[0][:, :]).then_inc(sq_added, 1)
            else:
                e.wait_ge(sq_added, 8 * r + k)
                e.tensor_tensor(into[:, :], into[:, :], buf[k % 2][:, :], ALU.add).then_inc(sq_added, 1)

        def as_seq(a):
            return a.rearrange("p k (n t) -> p k n t", t=TS_)

        def per_seq(a):
            return a.unsqueeze(3).to_broadcast([P, KD, NS, TS_])

        def dve_gain(e, ch, p_gain, q_scale):
            ch(e.tensor_scalar(gain[:, :, :], mod[:, q_scale:q_scale + 8, :], 1.0, None, ALU.add))
            ch(e.tensor_tensor(gain[:, :, :], gain[:, :, :],
                               prm[:, p_gain:p_gain + 8].unsqueeze(2).to_broadcast([P, KD, 9]), ALU.mult))

        def dve_ada(e, ch, a, q_shift, buf):
            nb = len(buf)
            for k in range(KD):
                if k >= nb:
                    e.wait_ge(h_ready[k % 2], 4 * a + (k - nb) // 2 + 1)
                e.tensor_tensor(buf[k % nb][:, 0:TP], x[:, k, 0:TP], rstd[:, 0:TP], ALU.mult).then_inc(h_pre, 1)
                if k == 0:
                    ch(e.tensor_tensor(tsam[:, :, :], x[:, :, TP:T],
                                       rstd[:, TP:T].unsqueeze(1).to_broadcast([P, KD, TSAM]), ALU.mult))
                    ch(e.tensor_tensor(as_seq(tsam), as_seq(tsam), per_seq(gain[:, :, 1:9]), ALU.mult))
                    ch(e.tensor_tensor(as_seq(tsam), as_seq(tsam), per_seq(mod[:, q_shift:q_shift + 8, 1:9]), ALU.add))
                e.tensor_copy(buf[k % nb][:, TP:T], tsam[:, k, :]).then_inc(h_smp, 1)
                if k % 2 == 0 and k > 0:
                    split_lo(e, a, k - 1, buf)
            split_lo(e, a, KD - 1, buf)

        def act_ada(e, a, q_shift, buf):
            nb = len(buf)
            for k in range(KD):
                e.wait_ge(h_pre, 8 * a + k + 1)
                nc.scalar.activation(buf[k % nb][:, 0:TP], buf[k % nb][:, 0:TP], ACT.Identity,
                                     scale=gain[:, k, 0:1], bias=mod[:, q_shift + k, 0:1]).then_inc(h_aff, 1)
                e.wait_ge(h_aff, 8 * a + k + 1)
                e.wait_ge(h_smp, 8 * (a - (a > 1)) + k + 1)
                nc.scalar.copy(h_hi[:, k, :], buf[k % nb][:, :]).then_inc(h_hi_done, 1)

        def split_lo(e, a, k, buf):
            e.wait_ge(h_hi_done, 8 * a + k + 1)
            e.tensor_tensor(h_lo[:, k, :], buf[k % len(buf)][:, :], h_hi[:, k, :].bitcast(F), ALU.subtract
                            ).then_inc(h_ready[k % 2], 1)

        def pool_lo(e, a, buf):
            for k in range(0, KD, 2):
                split_lo(e, a, k, buf)

        def act_result(e, need, b, tbuf, gate0, bias0, bias1, free_need):
            e.wait_ge(*need)
            if free_need is not None:
                e.wait_ge(x_final, free_need)
            kw = dict(bias=bias0) if bias0 is not None else {}
            for c in range(NC):
                w = CW if c < 2 else TP - 2 * CW
                nc.scalar.activation(tbuf[:, c * CW:c * CW + w], bank[3 * b + c][:, 0:w], ACT.Identity,
                                     scale=gate0, **kw)
            kw = dict(bias=bias1) if bias1 is not None else {}
            nc.scalar.activation(tbuf[:, TP:T], bank[3 * b + 2][:, TP - 2 * CW:CW], ACT.Identity,
                                 **kw).then_inc(job_free[b], 1)

        def dve_result(e, ch, need, tbuf, gates, xm):
            e.wait_ge(*need)
            ts = tbuf[:, TP:T].rearrange("p (n t) -> p n t", t=TS_)
            ch(e.tensor_tensor(ts, ts, gates.unsqueeze(2).to_broadcast([P, NS, TS_]), ALU.mult))
            e.tensor_tensor(xm, xm, tbuf[:, :], ALU.add).then_inc(x_final, 1)

        c_sem, mean_col = sem("c_silu"), sem("mean_col")
        hist_in, cap_out = [sem(f"hist_in{i}") for i in range(2)], [sem(f"cap_out{i}") for i in range(2)]
        conv_done, ln_dve = sem("conv_done"), sem("ln_dve")
        conv_half = [sem(f"conv_half{i}") for i in range(2)]
        centred = sem("centred")
        FF = [dict(conv=[sem(f"f{l}_conv{w}") for w in range(2)], op1=[sem(f"f{l}_op1{w}") for w in range(2)],
                   silu=sem(f"f{l}_silu"), mul=sem(f"f{l}_mul"), zh=sem(f"f{l}_zh"), zl=sem(f"f{l}_zl"),
                   dn=sem(f"f{l}_down"), load=sem(f"f{l}_load"), load2=sem(f"f{l}_load2"), state=sem(f"f{l}_state"), zero=sem(f"f{l}_zero"),
                   dve=sem(f"f{l}_dve")) for l in range(2)]
        copies = sem("copies")
        out_sem, y_ready = sem("out_sem"), sem("y_ready")
        JB = {"w1": 0, "w2": 8, "ffn0": 12, "k": 78, "q": 84, "wo": 87, "ffn1": 91}
        XB = {"w2": 0, "ffn0": 8, "wo": 96, "ffn1": 104}

        def cache_rows(g, n):
            w = SPAN * DIL[g] * 512
            cut = TS_ * 512
            return ins[f"cache{g}"][bass.ds(n, 1)].rearrange("o m -> (o m)")[cut:w].rearrange("(a b) -> a b", a=P)

        def sp_ffn(e, l):
            ph = f"ffn{l}"
            ff = FF[l]
            need = (h_pre, 8 * (2 if l == 0 else 5) + 8)

            def ups(n, k):
                for w in range(2):
                    fetch(e, ph, w, n + w, k)

            ups(0, 0)
            e.wait_ge(*need)
            e.dma_start(cwb[:, :, :], ins["cwb"][l]).then_inc(ff["load"], 16)
            e.dma_start(hist[:, :, :], ins["hist_f"][l]).then_inc(ff["load2"], 16)
            for s in (D0, D1):
                fetch(e, ph, s, s, 0)

            def group(f):
                ups(6 * f - 2, 2 * f - 1)
                for s in (D0, D1):
                    fetch(e, ph, s, 6 * f + s - D0, f)
                ups(6 * f + 2, 2 * f)

            if l == 0:
                with e.Fori(1, 1 + NS) as f:
                    group(f)
                    for g in range(3):
                        e.dma_start(outs[f"kvs{g}"][bass.ds(f - 1, 1)].rearrange("o (a b) -> (o a) b", a=P),
                                    cache_rows(g, f - 1)).then_inc(copies, 16)
                with e.Fori(1 + NS, NG) as f:
                    group(f)
            else:
                with e.Fori(1, NG) as f:
                    group(f)
            for s in (D0, D1):
                fetch(e, ph, s, 6 * NG - 2 + s - D0, NG)

        kst_out, vst_out = [sem(f"kst_out{i}") for i in range(2)], [sem(f"vst_out{i}") for i in range(4)]
        v_done, v_free, cfo_out = sem("v_done"), [sem(f"v_free{i}") for i in range(2)], [sem(f"cfo_out{i}") for i in range(2)]
        zset, zero_out = sem("zeros_set"), sem("zero_out")
        att_in = [sem(f"att_in{i}") for i in range(8)]
        b_in = [sem(f"bias_in{i}") for i in range(4)]
        att_used = [sem(f"att_used{s}") for s in range(4)]
        at_ = {x: sem(f"att_{x}") for x in (
            "qd", "sc", "ss", "st", "smax", "sexp", "sp", "sb", "spc", "osam", "s_done", "s_free", "nm", "exp", "p", "t_done",
            "pt", "pv", "o_free", "ln", "lse", "lb", "ls", "sub", "e", "w", "z", "hi", "o_ready", "chain")}
        PREV = [[b > 0 for b in range(8)], [b % 2 == 1 for b in range(8)], [False] * 8]

        def branch_view(a, g, lo, hi):
            d = DIL[g]
            return a[:, 0:TP].rearrange("p (r i) -> p r i", r=d)[:, :, lo // d:hi // d]

        def as_residues(a, g):
            return a.rearrange("p (i r) -> p r i", r=DIL[g])

        block = enter(nc.Block())

        @block.sync
        def _(e):
            e.dma_start(cact[:, :, :], ins["ct"]).then_inc(params[0], 16)
            e.dma_start(prm[:, :], ins["prm"]).then_inc(params[1], 16)
            e.dma_start(ident[:, :], ins["ident"]).then_inc(params[2], 16)
            mod_fetch(e, 0)
            for hf in range(4):
                e.dma_start(x[:, 2 * hf:2 * hf + 2, :], ins["xt"][:, 2 * hf:2 * hf + 2, :]).then_inc(xload[hf], 16)
            for g in range(1, 4):
                mod_fetch(e, g)
                if g == 1:
                    for s in (A0, A1):
                        fetch(e, "w1", s, s, 0, first=True)
                    for mm in range(2):
                        e.dma_start(full[mm][:, FS:FL].rearrange("p (n r) -> p n r", r=FSEG)[:, :, 0:HA],
                                    ins["hist_a"][mm].rearrange("p (n r) -> p n r", r=HA)).then_inc(hist_in[mm], 16)

            e.wait_ge(zset, 1)
            for r in range(4):
                e.dma_start(outs["kvz"][r], zeros[:, :]).then_inc(zero_out, 16)

            def state_out(m, b, i):
                e.wait_ge(job_free[1], m + 1)
                cap = outs["cap"][m] if isinstance(m, int) else outs["cap"][bass.ds(m, 1)].rearrange("o p n -> p (o n)")
                e.dma_start(cap[:, 0:HA], full[b][:, TP:TP + HA]).then_inc(cap_out[b], 16)
                e.wait_ge(cap_out[b], 32 * i + 16)
                e.dma_start(cap[:, HA:HA * 9].rearrange("p (n r) -> p n r", r=HA),
                            full[b][:, FS:FL].rearrange("p (n r) -> p n r", r=FSEG)[:, :, TS_:FSEG]).then_inc(cap_out[b], 16)
                e.wait_ge(cap_out[b], 32 * i + 32)

            def w1_units(i):
                for mm in range(2):
                    k = 2 * i + mm
                    if not (isinstance(k, int) and k == 0):
                        fetch(e, "w1", A0, 2 * k, k)
                        fetch(e, "w1", A1, 2 * k + 1, k)
                    for j in range(2):
                        mod_fetch(e, 2 * k + 4 + j)
                        if j == 0 and not isinstance(i, int):
                            state_out(k - 2, mm, i - 1)
                            e.wait_ge(conv_done, k - 1)
                            e.dma_start(full[mm][:, FS:FL].rearrange("p (n r) -> p n r", r=FSEG)[:, :, 0:HA],
                                        ins["hist_a"][bass.ds(k, 1)].rearrange("o p (n r) -> p (o n) r", r=HA)
                                        ).then_inc(hist_in[mm], 16)

            w1_units(0)
            with e.Fori(1, 4) as i:
                w1_units(i)
            for g in range(20, 24):
                mod_fetch(e, g)
                if g < 22:
                    state_out(g - 14, g - 20, 3)
            for s in (A0, A1):
                fetch(e, "w2", s, s, 0)
            for g in range(24, 28):
                mod_fetch(e, g)
            e.wait_ge(turned, 28)
            for s in (D0, D1):
                fetch(e, "w2", s, s, 0, first=True)
            for s in range(4):
                fetch(e, "w2", s, 4 + s, 1)
            sp_ffn(e, 0)
            def kv_fetch(c):
                fetch(e, "kv", c % 4, c, c // 4)

            for c in range(8):
                kv_fetch(c)
            e.wait_ge(FF[0]["state"], 2 * NJ)
            e.dma_start(outs["cfo"][0], ostate[:, :, :]).then_inc(cfo_out[0], 16)
            for c in range(6):
                e.wait_ge(job_free[c % 2], JB["k"] + c // 2 + 1)
                e.dma_start(outs["kt"][c], kst[c % 2][:, :]).then_inc(kst_out[c % 2], 16)
                if c < 4:
                    kv_fetch(8 + c)
            for n in range(18):
                c, part = n // 3, n % 3
                e.wait_ge(v_free[n % 2], n // 2 + 1)
                cs = slice(c * P, (c + 1) * P)
                if part < 2:
                    e.dma_start(outs["v"][512 * part:512 * part + 512, cs].rearrange("(b p) n -> p b n", p=P),
                                vst[n % 4][:, :, :]).then_inc(vst_out[n % 4], 16)
                else:
                    e.dma_start(outs["v"][TP:T, cs], vst[n % 4][0:TSAM, 0, :]).then_inc(vst_out[n % 4], 16)
                if n == 8:
                    for s in (A0, A1):
                        fetch(e, "q", s, s, 0)
            for c in range(2, 6):
                fetch(e, "q", c % 4, c, c // 4)

            def att_unit(n):
                s, k = n % 4, n // 4
                if k == 0:
                    e.wait_ge(split[s], n_split("att", s, 0))
                else:
                    e.wait_ge(att_used[s], k)
                e.dma_start(w_raw[s][:, :], ins["att"][n]).then_inc(landed[s], 16)

            for n in range(4):
                att_unit(n)
            for s in (A0, A1):
                e.wait_ge(used[s], n_split("q", s, 1) + 1)
            for b in range(2):
                e.wait_ge(kst_out[b], 48)
            for b in range(4):
                e.wait_ge(vst_out[b], 16 * (5 if b < 2 else 4))
            e.dma_start(kt[:, :, :], outs["kt"].rearrange("c p t -> p c t")).then_inc(att_in[0], 16)
            v = outs["v"]
            e.dma_start(v_sb[0][:, :, :], v[0:TP, 0:256].rearrange("(b p) n -> p b n", p=P)).then_inc(att_in[1], 16)
            e.dma_start(vn[:, :], v[TP:T, :]).then_inc(att_in[2], 16)
            e.dma_start(bsam[:, :, :], ins["bias_s"]).then_inc(att_in[3], 16)

            def load_bias(n):
                e.dma_start(btab[:, n % 4, :, :], ins["bias_p"][n]).then_inc(b_in[n % 4], 16)

            for n in range(4):
                load_bias(n)

            for n in range(4, 8):
                att_unit(n)
            e.dma_start(v_sb[1][:, :, :].rearrange("p (r b) n -> p r b n", r=4),
                        v[0:TP, 256:512].rearrange("(b p r) n -> p r b n", b=2, r=4)).then_inc(att_in[4], 16)
            for r in range(2):
                e.dma_start(v_sb[2][64 * r:64 * r + 64, :, :],
                            v[0:TP, 512:768].rearrange("(i b r) n -> r i b n", b=8, r=2)[r]).then_inc(att_in[5 + r], 16)
            for n in range(8, 22):
                att_unit(n)
            for n in (4, 5):
                e.wait_ge(at_["nm"], 2 * (n - 4) + 2)
                load_bias(n)
            for n in range(22, N_ATT):
                att_unit(n)
            for s in range(4):
                e.wait_ge(att_used[s], 9)
                fetch(e, "wo", s, s, 0)
            for s in range(4):
                fetch(e, "wo", s, 4 + s, 1)
            sp_ffn(e, 1)
            e.wait_ge(FF[1]["state"], 2 * NJ)
            e.dma_start(outs["cfo"][1], ostate[:, :, :]).then_inc(cfo_out[1], 16)
            for k in range(KD):
                e.wait_ge(y_ready, k + 1)
                e.dma_start(outs["yt"][:, k, :], x[:, k, :]).then_inc(out_sem, 16)
            e.wait_ge(out_sem, 16 * KD)
            e.wait_ge(copies, 16 * 3 * NS)
            for b in range(2):
                e.wait_ge(cfo_out[b], 16)
                e.wait_ge(cap_out[b], 128)
            e.wait_ge(zero_out, 64)

        def pool_ffn_first(e, l):
            for s in (A0, A1):
                put(e, f"ffn{l}", s, 0)

        def pool_ffn(e, l):
            ph, ff = f"ffn{l}", FF[l]

            def z_lo_part(j, zi):
                e.wait_ge(ff["zh"], j + 1)
                e.tensor_tensor(z_lo[zi][:, 0:TP], cv[1][:, 0:TP], z_hi[zi][:, 0:TP].bitcast(F), ALU.subtract)
                e.tensor_tensor(z_lo[zi][:, TP:T].rearrange("p (n t) -> p n t", t=TS_), cv_sam(cv[1]),
                                z_hi[zi][:, TP:T].bitcast(F).rearrange("p (n t) -> p n t", t=TS_), ALU.subtract
                                ).then_inc(ff["zl"], 1)

            for s in (D0, D1):
                put(e, ph, s, 0)
            z_lo_part(0, 0)
            with e.Fori(1, NG) as f:
                for a, d in ((A0, D0), (A1, D1)):
                    put(e, ph, d, f)
                    put(e, ph, a, 2 * f - 1)
                z_lo_part(2 * f - 1, 1)
                for s in (A0, A1):
                    put(e, ph, s, 2 * f)
                z_lo_part(2 * f, 0)
            for s in (D0, D1):
                put(e, ph, s, NG)
            z_lo_part(NJ - 1, 1)

        def cv_sam(c):
            return c[:, TP:TP + 6 * NS].rearrange("p (n r) -> p n r", r=6)[:, :, 2:2 + TS_]

        @block.gpsimd
        def _(e):
            e.memset(zeros[:, :], 0.0).then_inc(zset, 1)
            for s in (A0, A1):
                put(e, "w1", s, 0, first=True)
            pool_lo(e, 0, ada_bufs)

            def conv_part(m, b):
                own = m * (TS_ * 6)
                rows = full[b][:, FS:FL].rearrange("p (n r) -> p n r", r=FSEG)
                taps = prm[:, bass.ds(m * CA + P_DW, CA)].unsqueeze(1).to_broadcast([P, NS, CA])
                pool_wait(e, job_free[1], m + 1)
                for t in range(TS_):
                    e.tensor_tensor(scr, rows[:, :, t:t + CA], taps, ALU.mult).then_inc(pool_own, 1)
                    for step, half in enumerate((16, 8, 4, 2, 1)):
                        n = CA - 16 if half == 16 else half
                        e.wait_ge(pool_own, own + 6 * t + step + 1)
                        e.tensor_tensor(scr[:, :, 0:n] if half > 1 else ysmp[:, :, t:t + 1], scr[:, :, 0:n],
                                        scr[:, :, half:half + n], ALU.add).then_inc(pool_own, 1)
                    pool_wait(e, pool_own, own + 6 * t + 6)
                y = ycv[:, bass.ds(m, 1), :].rearrange("p o n -> p (o n)")
                e.tensor_tensor(y[:, TP:T], ysmp[:, :, :].rearrange("p n t -> p (n t)"),
                                prm[:, bass.ds(m + P_DWB, 1)].to_broadcast([P, TSAM]), ALU.add).then_inc(conv_smp, 1)
                e.wait_ge(conv_smp, m + 1)
                for hf in range(2):
                    pool_wait(e, conv_half[hf], CA * m + CA)
                e.tensor_tensor(ysum[:, :], ysum[:, :], y, ALU.add).then_inc(conv_done, 1)

            put(e, "w1", A0, 1)
            put(e, "w1", A1, 1)
            conv_part(0, 0)
            with e.Fori(0, 3) as i:
                for mm in range(2):
                    for s in (A0, A1):
                        put(e, "w1", s, 2 * i + mm + 2)
                    conv_part(2 * i + mm + 1, (mm + 1) % 2)
            conv_part(7, 1)
            for s in (A0, A1):
                put(e, "w2", s, 0)
            for s in range(4):
                e.wait_ge(mod_used[s], 28)
            pool_lo(e, 1, (mu, ysq))
            for s in (D0, D1):
                put(e, "w2", s, 0, first=True)
            for s in range(4):
                put(e, "w2", s, 1)
            pool_ffn_first(e, 0)
            pool_lo(e, 2, ada_bufs)
            pool_ffn(e, 0)
            for s in (A0, A1):
                put(e, "kv", s, 0)
            pool_lo(e, 3, ada_bufs)
            for s in (D0, D1):
                put(e, "kv", s, 0)
            for k in (1, 2):
                for s in range(4):
                    put(e, "kv", s, k)
            for s in (A0, A1):
                put(e, "q", s, 0)
            pool_lo(e, 4, tmp)
            for c in range(2, 6):
                put(e, "q", c % 4, c // 4)
            for j in range(2):
                if j == 1:
                    e.wait_ge(at_["z"], 3)
                    for s in (A0, A1):
                        put(e, "wo", s, 0)
                e.wait_ge(at_["o_free"], 3 * j + 3)
                for gg in range(3):
                    e.wait_ge(at_["e"], 3 * j + gg + 1)
                    e.tensor_tensor(orow[gg][:, :], orow[gg][:, :], mix[j][0][gg][:, :], ALU.mult
                                    ).then_inc(at_["w"], 1)
            e.wait_ge(at_["o_ready"], 8)
            for s in (D0, D1):
                put(e, "wo", s, 0)
            for s in range(4):
                put(e, "wo", s, 1)
            pool_ffn_first(e, 1)
            pool_lo(e, 5, ada_bufs)
            pool_ffn(e, 1)

        def act_ffn(e, l, q_gate, after_last):
            ph, ff, jb, xb = f"ffn{l}", FF[l], JB[f"ffn{l}"], XB[f"ffn{l}"]

            def up(j, w, job, first):
                ch = j + NJ * w
                cs = slice(ch, ch + 1) if isinstance(ch, int) else bass.ds(ch, 1)
                if isinstance(j, int) and j < 2:
                    s = (A0, D0)[j] + w
                    e.wait_ge(used[s], n_split(ph, s, 0) + 1)
                else:
                    e.wait_ge(used[A0 + w], n_split(ph, A0 + w, j))
                if not first:
                    e.wait_ge(ff["conv"][w], j)
                segs = u[w][:, 2 + TP:2 + UC].rearrange("p (n r) -> p n r", r=6)
                nc.scalar.copy(segs[:, :, 0:2], hist[:, cs, :].rearrange("p o (n r) -> p (o n) r", r=2))
                for c in range(NC):
                    w_ = CW if c < 2 else TP - 2 * CW
                    nc.scalar.copy(u[w][:, 2 + c * CW:2 + c * CW + w_], bank[3 * w + c][:, 0:w_])
                nc.scalar.copy(segs[:, :, 2:6], bank[3 * w + 2][:, TP - 2 * CW:CW].rearrange("p (n t) -> p n t", t=TS_)
                               ).then_inc(job_free[w], 1)
                e.wait_ge(job_free[w], job + 1)
                if not first:
                    if w == 0:
                        e.wait_ge(ff["mul"], j)
                    else:
                        e.wait_ge(ff["zl"], j)
                nc.scalar.activation(cv[w][:, :], u[w][:, 0:UC], ACT.Identity,
                                     scale=cwb[:, cs, 0:1].rearrange("p o n -> p (o n)"),
                                     bias=cwb[:, cs, 3:4].rearrange("p o n -> p (o n)")).then_inc(ff["op1"][w], 1)
                nc.scalar.copy(ostate[:, cs, :].rearrange("p o (n r) -> p (o n) r", r=2),
                               u[w][:, TP:TP + 54].rearrange("p (n r) -> p n r", r=6)[:, :, 0:2]
                               ).then_inc(ff["state"], 1)

            def ups(j, job, first=False):
                for w in range(2):
                    up(j, w, job, first)
                e.wait_ge(ff["conv"][0], j + 1)
                nc.scalar.activation(cv[0][:, :], cv[0][:, :], ACT.Silu).then_inc(ff["silu"], 1)

            def z_hi_part(j, zi, f):
                e.wait_ge(ff["mul"], j + 1)
                if f is not None:
                    e.wait_ge(used[D1], n_split(ph, D1, f) + 1)
                nc.scalar.copy(z_hi[zi][:, 0:TP], cv[1][:, 0:TP])
                nc.scalar.copy(z_hi[zi][:, TP:T].rearrange("p (n t) -> p n t", t=TS_), cv_sam(cv[1])).then_inc(ff["zh"], 1)

            def down(f):
                for m in range(KD):
                    need = (ff["dn"], 7 * f + m + 1) if m < 7 else (used[D1], n_split(ph, D1, f) + 2)
                    act_result(e, need, m % 2, tb[m % 2], mod[:, q_gate + m, 0:1], None, None, xb + 8 * f + m - 1)
                    if isinstance(f, int) and m >= 1:
                        after_last(m - 1)

            e.wait_ge(ff["load"], 16)
            e.wait_ge(ff["load2"], 16)
            e.wait_ge(ff["zero"], 1)
            ups(0, jb, True)
            z_hi_part(0, 0, None)
            ups(1, jb + 1)
            z_hi_part(1, 1, None)
            with e.Fori(1, NG) as f:
                ups(2 * f, 6 * f - 4 + jb)
                down(f - 1)
                z_hi_part(2 * f, 0, f)
                ups(2 * f + 1, 6 * f + 1 + jb)
                z_hi_part(2 * f + 1, 1, f)
            down(NG - 1)
            after_last(KD - 1)

        def act_branch(dst, c, g, scale):
            for b in range(NC):
                w = CW if b < 2 else TP - 2 * CW
                nc.scalar.activation(branch_view(dst, g, b * CW, b * CW + w), as_residues(bank[3 * (c % 2) + b][:, 0:w], g),
                                     ACT.Identity, scale=scale)
            nc.scalar.activation(dst[:, TP:T], bank[3 * (c % 2) + 2][:, TP - 2 * CW:CW], ACT.Identity, scale=scale
                                 ).then_inc(job_free[c % 2], 1)

        def act_attention(e):
            e.wait_ge(at_["smax"], 1)
            nc.scalar.activation(lsam[:, :, :], lsam[:, :, :], ACT.Exp, bias=cols[:, 1, 0:1], accum_out=cols[:, 2, 0:1]
                                 ).then_inc(at_["sexp"], 1)

            def exps(i):
                g = (i % 6) // 2
                e.wait_ge(at_["nm"], i + 1)
                for b in range(8):
                    lo = 0 if PREV[g][b] else P
                    last = nc.scalar.activation(lg[i % 2][:, b, lo:256], lg[i % 2][:, b, lo:256], ACT.Exp,
                                                bias=stat[:, 1, i, b:b + 1], accum_out=stat[:, 2, i, b:b + 1])
                last.then_inc(at_["exp"], 1)

            def weights(j):
                lse = mix[j][0]
                for gg in range(3):
                    e.wait_ge(at_["sub"], 3 * j + gg + 1)
                    nc.scalar.activation(lse[gg][:, :], lse[gg][:, :], ACT.Exp).then_inc(at_["e"], 1)

            def outputs(j):
                for gg in range(3):
                    e.wait_ge(at_["z"], 3 * j + gg + 1)
                    nc.scalar.copy(o_hi[:, 2 * gg + j, 0:TP], orow[gg][:, :]).then_inc(at_["hi"], 1)

            exps(0)
            for i in range(12):
                g, j = (i % 6) // 2, i // 6
                if i < 11:
                    exps(i + 1)
                for q in range(4):
                    n = 4 * i + q
                    e.wait_ge(at_["t_done"], n + 1)
                    if n >= 2:
                        e.wait_ge(at_["pv"], n - 1)
                    if g < 2:
                        lo = 0 if PREV[g][2 * q] else P
                        nc.scalar.copy(pt[n % 2][:, lo:512], bank[2 + n % 2][:, lo:512]).then_inc(at_["pt"], 1)
                    else:
                        nc.scalar.copy(pt[n % 2][:, :].rearrange("p (b k) -> p b k", b=2)[:, :, P:256],
                                       bank[2 + n % 2][:, :].rearrange("p (b k) -> p b k", b=2)[:, :, P:256]
                                       ).then_inc(at_["pt"], 1)
                if i % 6 == 5:
                    e.wait_ge(at_["exp"], i + 1)
                    nc.scalar.activation(stat[:, 2, 6 * j:6 * j + 6, :], stat[:, 2, 6 * j:6 * j + 6, :], ACT.Ln
                                         ).then_inc(at_["ln"], 1)
                    for n in range(6 * j, 6 * j + 6):
                        gg, hb = (n % 6) // 2, n % 2
                        e.wait_ge(at_["lb"], n + 1)
                        if n >= 6:
                            e.wait_ge(at_["o_ready"], 3)
                        d, lse = DIL[gg], mix[j][0]
                        if d == 1:
                            nc.scalar.copy(lse[gg][:, 512 * hb:512 * hb + 512], bank[6][:, :]).then_inc(at_["ls"], 1)
                        else:
                            nc.scalar.copy(as_residues(lse[gg][:, :], gg)[:, d // 2 * hb:d // 2 * (hb + 1), :],
                                           bank[6][:, :].rearrange("p (r i) -> p r i", r=d // 2)).then_inc(at_["ls"], 1)
                if i in (6, 11):
                    weights(i // 11)
                if i in (7, 11):
                    outputs(i // 11)

        @block.scalar
        def _(e):
            e.wait_ge(params[0], 16)
            nc.scalar.activation(cact[:, :, :], cact[:, :, :], ACT.Silu).then_inc(c_sem, 1)
            for k in range(KD):
                act_square(e, 0, k, x, sq, (xload[k // 2], 16))
            e.wait_ge(params[1], 16)
            take_rows(e, 0, 0)
            take_columns(e, 0)
            act_root(e, 0)
            act_wide(e, 0, rstd)
            for g in range(1, 4):
                take_rows(e, g, g % 2)
                take_columns(e, g)
            act_ada(e, 0, Q_SHM0, ada_bufs)
            def w1_act(i):
                for mm in range(2):
                    m = 2 * i + mm
                    e.wait_ge(used[A0], n_split("w1", A0, m) + 1)
                    if not (isinstance(m, int) and m == 0):
                        e.wait_ge(job_free[1], m)
                    for c in range(NC):
                        last = nc.scalar.activation(sg[:, c * CW:(c + 1) * CW], bank[c][:, 0:CW], ACT.Sigmoid,
                                                    bias=col(P_B1G, m))
                    last.then_inc(job_free[0], 1)
                    if not (isinstance(m, int) and m == 0):
                        take_columns(e, 2 * m + 3)
                    take_rows(e, 2 * m + 4, 0)
                    take_columns(e, 2 * m + 4)
                    take_rows(e, 2 * m + 5, 1)

            w1_act(0)
            with e.Fori(1, 4) as i:
                w1_act(i)
            take_columns(e, 19)
            for g in range(20, 25):
                take_rows(e, g, g % 2)
                take_columns(e, g)
            for b in range(2):
                e.wait_ge(cap_out[b], 128)
            act_wide(e, 1, mu)
            for k in range(KD):
                act_square(e, 1, k, ycv, tb, (centred, k + 1))
                if k in (3, 5, 7):
                    g = 25 + (k - 3) // 2
                    take_rows(e, g, g % 2)
                    take_columns(e, g)
            act_root(e, 1)
            act_wide(e, 2, rstd)
            for k in range(KD):
                e.wait_ge(h_pre, 8 + k + 1)
                if k >= 2:
                    e.wait_ge(h_ready[k % 2], 4 + k // 2)
                nc.scalar.activation((mu, ysq)[k % 2][:, :], ycv[:, k, :], ACT.Silu, scale=col(P_LNG, k),
                                     bias=col(P_LNB, k)).then_inc(h_aff, 1)
                e.wait_ge(h_aff, 8 + k + 1)
                nc.scalar.copy(h_hi[:, k, :], (mu, ysq)[k % 2][:, :]).then_inc(h_hi_done, 1)
            for m in range(KD):
                s = m % 4
                act_result(e, (used[s], n_split("w2", s, m // 4) + 1), m % 2, tb[m % 2], mod[:, Q_GM0 + m, 0:1],
                           b2g[:, m:m + 1], col(P_B2, m), m - 1 if m >= 2 else None)
                if m >= 1:
                    act_square(e, 2, m - 1, x, sq, (x_final, m))
            act_square(e, 2, 7, x, sq, (x_final, 8))
            act_root(e, 2)
            act_wide(e, 3, rstd)
            act_ada(e, 2, Q_SHF0, ada_bufs)
            act_ffn(e, 0, Q_GF0, lambda m: act_square(e, 3, m, x, sq, (x_final, 88 + m + 1)))
            act_root(e, 3)
            act_wide(e, 4, rstd)
            act_ada(e, 3, Q_SHKV, ada_bufs)
            for c in range(12):
                e.wait_ge(used[c % 4], n_split("kv", c % 4, c // 4) + 1)
                if 2 <= c < 8:
                    e.wait_ge(kst_out[c % 2], 16 * (c // 2))
                elif c >= 8:
                    e.wait_ge(v_done, 3 * (c - 7))
                act_branch(kst[c % 2], c, c // 2 if c < 6 else 0, 1.0)
            act_ada(e, 4, Q_SHM1, tmp)
            e.wait_ge(v_done, 18)
            for c in range(6):
                e.wait_ge(used[c % 4], n_split("q", c % 4, c // 4) + 1)
                act_branch(qt[:, c, :], c, c // 2, 0.125)
            act_attention(e)
            for m in range(KD):
                s = m % 4
                act_result(e, (used[s], n_split("wo", s, m // 4) + 1), m % 2, tb[m % 2], mod[:, Q_GM1 + m, 0:1],
                           None, None, XB["wo"] + m - 1 if m >= 2 else None)
                if m >= 1:
                    act_square(e, 4, m - 1, x, sq, (x_final, XB["wo"] + m))
            act_square(e, 4, 7, x, sq, (x_final, XB["wo"] + 8))
            act_root(e, 4)
            act_wide(e, 5, rstd)
            act_ada(e, 5, Q_SHF1, ada_bufs)
            act_ffn(e, 1, Q_GF1, lambda m: act_square(e, 5, m, x, sq, (x_final, XB["ffn1"] + 80 + m + 1)))
            act_root(e, 5)
            act_wide(e, 6, rstd)

        def dve_ffn(e, l, q_gate, r):
            ph, ff, jb, xb = f"ffn{l}", FF[l], JB[f"ffn{l}"], XB[f"ffn{l}"]

            def convs(j, ch):
                cb = j if isinstance(j, int) else None
                for w in range(2):
                    c0 = j + NJ * w
                    cs = slice(c0, c0 + 1) if cb is not None else bass.ds(c0, 1)
                    e.wait_ge(ff["op1"][w], j + 1)
                    ch(e.scalar_tensor_tensor(cv[w][:, :], u[w][:, 1:1 + UC], cwb[:, cs, 1:2].rearrange("p o n -> p (o n)"),
                                              cv[w][:, :], ALU.mult, ALU.add))
                    e.scalar_tensor_tensor(cv[w][:, :], u[w][:, 2:2 + UC], cwb[:, cs, 2:3].rearrange("p o n -> p (o n)"),
                                           cv[w][:, :], ALU.mult, ALU.add).then_inc(ff["conv"][w], 1)
                e.wait_ge(ff["silu"], j + 1)
                e.wait_ge(ff["conv"][1], j + 1)
                e.tensor_tensor(cv[1][:, :], cv[0][:, :], cv[1][:, :], ALU.mult).then_inc(ff["mul"], 1)

            def down(f, ch, last=False):
                for m in range(KD):
                    dve_result(e, ch, (job_free[m % 2], 6 * f + jb + 4 + m // 2 - (1 if last else 0)), tb[m % 2],
                               mod[:, q_gate + m, 1:9], x[:, m, :])
                    if last and m >= 1:
                        dve_add_square(e, r, m - 1, sq, acc)

            e.memset(u[0][:, 0:2], 0.0)
            e.memset(u[1][:, 0:2], 0.0).then_inc(ff["zero"], 1)
            ch = Chain(e, ff["dve"])
            convs(0, ch)
            convs(1, ch)
            assert ch.n == 4
            with e.Fori(1, NG) as f:
                ch = Chain(e, ff["dve"], 12 * f - 8)
                convs(2 * f, ch)
                down(f - 1, ch)
                convs(2 * f + 1, ch)
            ch = Chain(e, ff["dve"], 12 * NG - 8)
            down(NG - 1, ch, last=True)
            dve_add_square(e, r, KD - 1, sq, acc)

        def dve_attention(e):
            ch = Chain(e, at_["chain"])
            for b in range(2):
                e.wait_ge(job_free[b], JB["q"] + 3)
            ch(e.memset(qd[:, :, :, :], 0.0))
            e.tensor_copy(qd[0:64, :, :, 0], qt[0:64, :, TP:T])
            e.tensor_copy(qd[64:P, :, :, 1], qt[64:P, :, TP:T]).then_inc(at_["qd"], 1)
            e.wait_ge(at_["sc"], 1)
            e.tensor_copy(s_sb[:, :], bank[0][:, 0:384])
            e.tensor_copy(sn_sb[:, :], bank[1][0:TSAM, 0:384]).then_inc(at_["ss"], 1)
            e.wait_ge(at_["st"], 1)
            e.wait_ge(att_in[3], 16)
            for g in range(3):
                last = e.tensor_tensor_reduce(lsam[:, g, :], bank[2][:, 160 * g:160 * g + 160], bsam[:, g, :], 1.0, NEG,
                                              ALU.add, ALU.max, cols[:, 0, g:g + 1])
            ch(last)
            ch(e.tensor_reduce(cols[:, 0, 3:4], cols[:, 0, 0:3], AX, ALU.max))
            e.tensor_scalar(cols[:, 1, 0:1], cols[:, 0, 3:4], -1.0, None, ALU.mult).then_inc(at_["smax"], 1)
            e.wait_ge(at_["sexp"], 1)
            ch(e.reciprocal(cols[:, 3, 0:1], cols[:, 2, 0:1]))
            e.tensor_scalar(lsam[:, :, :], lsam[:, :, :], cols[:, 3, 0:1], None, ALU.mult).then_inc(at_["sp"], 1)
            e.wait_ge(at_["sb"], 1)
            e.tensor_copy(pc[:, :], bank[3][:, 0:384])
            e.tensor_copy(pn[:, :], bank[0][0:TSAM, 0:384]).then_inc(at_["spc"], 1)

            def logits(i):
                g, hp, bt = (i % 6) // 2, i % 2, i // 2
                if hp == 0:
                    e.wait_ge(b_in[bt % 4], 16 * (bt // 4) + 16)
                if i >= 2:
                    e.wait_ge(at_["t_done"], 4 * i - 4)
                for q in range(4):
                    e.wait_ge(at_["s_done"], 4 * i + q + 1)
                    for b in (2 * q, 2 * q + 1):
                        lo = 0 if PREV[g][b] else P
                        last = e.tensor_tensor_reduce(
                            lg[i % 2][:, b, lo:256], bank[q % 2][:, (b % 2) * 256 + lo:(b % 2) * 256 + 256],
                            btab[:, bt % 4, hp, lo:256], 1.0, NEG, ALU.add, ALU.max, stat[:, 0, i, b:b + 1])
                    last.then_inc(at_["s_free"], 1)
                e.wait_ge(at_["s_free"], 4 * i + 4)
                e.tensor_scalar(stat[:, 1, i, :], stat[:, 0, i, :], -1.0, None, ALU.mult).then_inc(at_["nm"], 1)

            def weights(j):
                lse, top, _ = mix[j]
                e.wait_ge(at_["ls"], 6 * j + 6)
                ch(e.tensor_tensor(top[:, :], lse[0][:, :], lse[1][:, :], ALU.max))
                ch(e.tensor_tensor(top[:, :], top[:, :], lse[2][:, :], ALU.max))
                for gg in range(3):
                    e.tensor_tensor(lse[gg][:, :], lse[gg][:, :], top[:, :], ALU.subtract).then_inc(at_["sub"], 1)

            def outputs(j):
                lse, _, rz = mix[j]
                e.wait_ge(at_["e"], 3 * j + 2)
                ch(e.tensor_tensor(rz[:, :], lse[0][:, :], lse[1][:, :], ALU.add))
                e.wait_ge(at_["e"], 3 * j + 3)
                ch(e.tensor_tensor(rz[:, :], rz[:, :], lse[2][:, :], ALU.add))
                ch(e.reciprocal(rz[:, :], rz[:, :]))
                for gg in range(3):
                    e.wait_ge(at_["w"], 3 * j + gg + 1)
                    e.tensor_tensor(orow[gg][:, :], orow[gg][:, :], rz[:, :], ALU.mult).then_inc(at_["z"], 1)
                for gg in range(3):
                    e.wait_ge(at_["hi"], 3 * j + gg + 1)
                    e.tensor_tensor(o_lo[:, 2 * gg + j, 0:TP], orow[gg][:, :], o_hi[:, 2 * gg + j, 0:TP].bitcast(F),
                                    ALU.subtract).then_inc(at_["o_ready"], 1)

            logits(0)
            for i in range(12):
                g, hp, j = (i % 6) // 2, i % 2, i // 6
                if i < 11:
                    logits(i + 1)
                e.wait_ge(at_["exp"], i + 1)
                ch(e.reciprocal(rsum[:, i, :], stat[:, 2, i, :]))
                for b in range(8):
                    lo = 0 if PREV[g][b] else P
                    e.tensor_scalar(lg[i % 2][:, b, lo:256], lg[i % 2][:, b, lo:256], rsum[:, i, b:b + 1], None,
                                    ALU.mult).then_inc(at_["p"], 1)
                if i == 6:
                    weights(0)
                if i == 7:
                    outputs(0)
                if hp == 1:
                    e.wait_ge(at_["pv"], 4 * i + 4)
                    if j == 1:
                        e.wait_ge(at_["o_ready"], 3)
                    d = DIL[g]
                    for hb in range(2):
                        src = bank[4 + hb][:, :]
                        if d == 1:
                            last = e.tensor_copy(orow[g][:, 512 * hb:512 * hb + 512], src)
                        else:
                            last = e.tensor_copy(as_residues(orow[g][:, :], g)[:, d // 2 * hb:d // 2 * (hb + 1), :],
                                                 src.rearrange("p (r i) -> p r i", r=d // 2))
                    last.then_inc(at_["o_free"], 1)
                if i % 6 == 5:
                    e.wait_ge(at_["ln"], j + 1)
                    e.tensor_tensor(stat[:, 2, 6 * j:6 * j + 6, :], stat[:, 2, 6 * j:6 * j + 6, :],
                                    stat[:, 0, 6 * j:6 * j + 6, :], ALU.add).then_inc(at_["lse"], 1)
                    if j == 1:
                        e.wait_ge(at_["osam"], 1)
                        ov = bank[7][:, 0:384].rearrange("p (c t h) -> p c t h", c=6, h=2)
                        e.tensor_copy(osam[0:64, :, :], ov[0:64, :, :, 0])
                        ch(e.tensor_copy(osam[64:P, :, :], ov[64:P, :, :, 1]))
                        e.tensor_copy(o_hi[:, :, TP:T], osam[:, :, :]).then_inc(at_["o_ready"], 1)
                        e.wait_ge(at_["o_ready"], 4)
                        e.tensor_tensor(o_lo[:, :, TP:T], osam[:, :, :], o_hi[:, :, TP:T].bitcast(F), ALU.subtract
                                        ).then_inc(at_["o_ready"], 1)
                    if j == 1:
                        weights(1)
                        outputs(1)

        @block.vector
        def _(e):
            ch = Chain(e, dve)
            e.memset(ones[:, :], 1.0).then_inc(consts, 1)
            for b in range(2):
                e.memset(full[b][:, 0:HA], 0.0)
            for k in range(KD):
                dve_add_square(e, 0, k, sq, tb[1])
            dve_inverse_root(e, ch, 0, 0, EPS)
            e.wait_ge(mod_done, 4)
            e.wait_ge(params[1], 16)
            dve_gain(e, ch, P_NM0, Q_SCM0)
            e.wait_ge(wide_sb, 1)
            dve_ada(e, ch, 0, Q_SHM0, ada_bufs)
            ch(e.memset(ysum[:, :], 0.0))

            e.wait_ge(zero_out, 64)
            with e.Fori(0, 4) as i:
                for b in range(2):
                    m = 2 * i + b
                    fb = full[b]
                    e.wait_ge(hist_in[b], 16 * i + 16)
                    e.wait_ge(job_free[0], m + 1)
                    e.wait_ge(used[A1], n_split("w1", A1, m) + 1)
                    b1 = col(P_B1A, m)
                    for c in range(NC):
                        w = CW if c < 2 else TP - 2 * CW
                        e.scalar_tensor_tensor(fb[:, HA + c * CW:HA + c * CW + w], bank[3 + c][:, 0:w], b1,
                                               sg[:, c * CW:c * CW + w], ALU.add, ALU.mult)
                    rows = fb[:, FS:FL].rearrange("p (n r) -> p n r", r=FSEG)
                    e.scalar_tensor_tensor(rows[:, :, HA:FSEG],
                                           bank[5][:, TP - 2 * CW:CW].rearrange("p (n t) -> p n t", t=TS_), b1,
                                           sg[:, TP:T].rearrange("p (n t) -> p n t", t=TS_), ALU.add, ALU.mult
                                           ).then_inc(job_free[1], 1)
                    e.wait_ge(job_free[1], m + 1)
                    y = ycv[:, bass.ds(m, 1), :].rearrange("p o n -> p (o n)")
                    for w in range(CA):
                        tap = prm[:, bass.ds(m * CA + P_DW + w, 1)]
                        for hf in range(2):
                            t0, t1 = hf * TP // 2, (hf + 1) * TP // 2
                            if w == 0:
                                last = e.tensor_scalar(y[:, t0:t1], fb[:, t0:t1], tap, col(P_DWB, m), ALU.mult, ALU.add)
                            else:
                                e.wait_ge(conv_half[hf], CA * m + w)
                                last = e.scalar_tensor_tensor(y[:, t0:t1], fb[:, w + t0:w + t1], tap, y[:, t0:t1],
                                                              ALU.mult, ALU.add)
                            last.then_inc(conv_half[hf], 1)
            ch = Chain(e, ln_dve)
            e.wait_ge(col_sum, 2)
            e.tensor_scalar(cols[:, 0, :], bank[6][:, 0:9], 1.0 / D, None, ALU.mult).then_inc(mean_col, 1)
            e.wait_ge(mod_done, 24)
            ch(e.tensor_tensor(b2g[:, :], prm[:, P_B2:P_B2 + 8], mod[:, Q_GM0:Q_GM0 + 8, 0:1].rearrange("p k o -> p (k o)"),
                               ALU.mult))
            dve_gain(e, ch, P_NF0, Q_SCF0)
            e.wait_ge(wide_sb, 2)
            for k in range(KD):
                e.tensor_tensor(ycv[:, k, :], ycv[:, k, :], mu[:, :], ALU.subtract).then_inc(centred, 1)
                if k >= 1:
                    dve_add_square(e, 1, k - 1, tb, ysq)
            dve_add_square(e, 1, 7, tb, ysq)
            dve_inverse_root(e, ch, 1, 2, LN_EPS)
            e.wait_ge(wide_sb, 3)
            for k in range(KD):
                e.wait_ge(centred, 8)
                e.tensor_tensor(ycv[:, k, :], ycv[:, k, :], rstd[:, :], ALU.mult).then_inc(h_pre, 1)
                if k >= 2 and k % 2 == 0:
                    split_lo(e, 1, k - 1, (mu, ysq))
            split_lo(e, 1, 7, (mu, ysq))
            for m in range(KD):
                dve_result(e, ch, (job_free[m % 2], 8 + m // 2 + 1), tb[m % 2], mod[:, Q_GM0 + m, 1:9], x[:, m, :])
                if m >= 1:
                    dve_add_square(e, 2, m - 1, sq, acc)
            dve_add_square(e, 2, 7, sq, acc)
            dve_inverse_root(e, ch, 2, 3, EPS)
            e.wait_ge(wide_sb, 4)
            dve_ada(e, ch, 2, Q_SHF0, ada_bufs)
            dve_ffn(e, 0, Q_GF0, 3)
            dve_inverse_root(e, ch, 3, 4, EPS)
            dve_gain(e, ch, P_NKV, Q_SCKV)
            e.wait_ge(wide_sb, 5)
            dve_ada(e, ch, 3, Q_SHKV, ada_bufs)
            e.wait_ge(h_hi_done, 32)
            dve_gain(e, ch, P_NM1, Q_SCM1)
            e.wait_ge(cfo_out[0], 16)
            for n in range(18):
                e.wait_ge(v_done, n + 1)
                if n >= 4:
                    e.wait_ge(vst_out[n % 4], 16 * (n // 4))
                if n % 3 < 2:
                    last = e.tensor_copy(vst[n % 4][:, :, :].rearrange("p b n -> p (b n)"), bank[6 + n % 2][:, :])
                else:
                    last = e.tensor_copy(vst[n % 4][0:TSAM, 0, :], bank[6 + n % 2][0:TSAM, 0:P])
                last.then_inc(v_free[n % 2], 1)
            dve_ada(e, ch, 4, Q_SHM1, tmp)
            e.wait_ge(h_hi_done, 40)
            dve_gain(e, ch, P_NF1, Q_SCF1)
            dve_attention(e)
            for m in range(KD):
                dve_result(e, ch, (job_free[m % 2], JB["wo"] + m // 2 + 1), tb[m % 2], mod[:, Q_GM1 + m, 1:9], x[:, m, :])
                if m >= 1:
                    dve_add_square(e, 4, m - 1, sq, acc)
            dve_add_square(e, 4, 7, sq, acc)
            dve_inverse_root(e, ch, 4, 5, EPS)
            e.wait_ge(wide_sb, 6)
            dve_ada(e, ch, 5, Q_SHF1, ada_bufs)
            dve_ffn(e, 1, Q_GF1, 5)
            dve_inverse_root(e, ch, 5, 6, EPS)
            e.wait_ge(wide_sb, 7)
            for k in range(KD):
                e.scalar_tensor_tensor(x[:, k, :], x[:, k, :], col(P_NFIN, k), rstd[:, :], ALU.mult, ALU.mult
                                       ).then_inc(y_ready, 1)

        def pe_ffn(e, l, a):
            ph, ff, jb = f"ffn{l}", FF[l], JB[f"ffn{l}"]

            def ups(k, job, s0=A0):
                for w in range(2):
                    product(e, ph, s0 + w, k, w, job, h_hi, h_lo)

            def down(f, job):
                e.wait_ge(split[D0], n_split(ph, D0, f) + 2)
                e.wait_ge(split[D1], n_split(ph, D1, f) + 2)

                def half(m, zi):
                    b, s = m % 2, D0 + zi
                    for q, (w, z) in enumerate(((w_hi, z_hi), (w_hi, z_lo), (w_lo, z_hi))):
                        for c in range(NC):
                            mm = e.matmul(bank[3 * b + c][:, 0:CW], w[s][:, m * P:(m + 1) * P],
                                          z[zi][:, c * CW:(c + 1) * CW], start=(zi == 0 and q == 0),
                                          stop=(zi == 1 and q == 2))
                    return mm

                ahead = 2 if isinstance(f, int) else 0
                if ahead:
                    e.wait_ge(ff["zl"], 2 * f + 1)
                    for m in range(ahead):
                        e.wait_ge(job_free[m], job)
                        half(m, 0)
                e.wait_ge(ff["zl"], 2 * f + 2)
                for m in range(KD):
                    if m >= ahead:
                        e.wait_ge(job_free[m % 2], job + m // 2)
                        mm = half(m, 0)
                        if m == KD - 1:
                            mm.then_inc(used[D0], 1)
                    mm = half(m, 1)
                    mm.then_inc(ff["dn"] if m < KD - 1 else used[D1], 1)

            product_pair(e, ph, jb, a)
            ups(0, jb + 1, D0)
            with e.Fori(0, (NG - 1) // 2) as i:
                for f in (2 * i + 1, 2 * i + 2):
                    ups(2 * f - 1, 6 * f + (jb - 4))
                    down(f - 1, 6 * f + (jb - 3))
                    ups(2 * f, 6 * f + (jb + 1))
            down(NG - 1, 6 * NG - 4 + jb)

        def pe_attention(e):
            e.wait_ge(at_["qd"], 1)
            for n in range(18):
                s, k = n % 4, n // 4
                e.wait_ge(landed[s], 16 * (n_land("att", s, k) + 1))
                for pr in range(2):
                    if n < 16:
                        g, q0 = 1 + n // 8, TS_ * (n % 8)
                        for t in range(TS_):
                            cc = ((2 * g + pr) * TSAM + q0 + t) * 2
                            mm = e.matmul(bank[0][:, cc:cc + 2], w_raw[s][:, (pr * TS_ + t) * P:(pr * TS_ + t + 1) * P],
                                          qd[:, 2 * g + pr, q0 + t, :], start=True, stop=True)
                    else:
                        for nn in range(4):
                            q0 = TS_ * (4 * (n - 16) + nn)
                            cc = (pr * TSAM + q0) * 2
                            mm = e.matmul(bank[0][:, cc:cc + 8], w_raw[s][:, (nn * 2 + pr) * P:(nn * 2 + pr + 1) * P],
                                          qd[:, pr, q0:q0 + TS_, :].rearrange("p t h -> p (t h)"), start=True, stop=True)
                mm.then_inc(att_used[s], 1)
            e.wait_ge(att_in[0], 16)
            for c in range(6):
                mm = e.matmul(bank[1][0:TSAM, 64 * c:64 * c + 64], kt[:, c, TP:T], qd[:, c, :, :].rearrange("p t h -> p (t h)"),
                              start=True, stop=True)
            mm.then_inc(at_["sc"], 1)
            e.wait_ge(at_["ss"], 1)
            for g in range(3):
                e.transpose(bank[2][:, 160 * g:160 * g + P], s_sb[:, P * g:P * g + P], ident[:, :])
                mm = e.transpose(bank[2][:, 160 * g + P:160 * g + 160], sn_sb[:, P * g:P * g + P], ident[0:TSAM, 0:TSAM])
            mm.then_inc(at_["st"], 1)
            e.wait_ge(at_["sp"], 1)
            for g in range(3):
                e.transpose(bank[3][:, P * g:P * g + P], lsam[:, g, 0:P], ident[:, :])
                mm = e.transpose(bank[0][0:TSAM, P * g:P * g + P], lsam[:, g, P:160], ident[:, :])
            mm.then_inc(at_["sb"], 1)
            e.wait_ge(at_["spc"], 1)
            e.wait_ge(att_in[2], 16)
            for c in range(6):
                e.matmul(bank[7][:, 64 * c:64 * c + 64], vn[:, P * c:P * c + P], pn[:, 64 * c:64 * c + 64],
                         start=(c == 0), stop=False, skip_group_check=True)

            def scores(i):
                g, hp, j = (i % 6) // 2, i % 2, i // 6
                c, r = 2 * g + j, slice(64 * hp, 64 * hp + 64)
                for q in range(4):
                    n = 4 * i + q
                    if n >= 2:
                        e.wait_ge(at_["s_free"], n - 1)
                    for b in (2 * q, 2 * q + 1):
                        pv = PREV[g][b]
                        lo = 0 if pv else P
                        mm = e.matmul(bank[q % 2][:, (b % 2) * 256 + lo:(b % 2) * 256 + 256], qt[r, c, b * P:b * P + P],
                                      kt[r, c, (b - pv) * P:(b + 1) * P], start=True, stop=True)
                    mm.then_inc(at_["s_done"], 1)

            def turn(i, q):
                g = (i % 6) // 2
                n = 4 * i + q
                e.wait_ge(at_["p"], 8 * i + 2 * q + 2)
                if n >= 2:
                    e.wait_ge(at_["pt"], n - 1)
                for b in (2 * q, 2 * q + 1):
                    for half in ((0, 1) if PREV[g][b] else (1,)):
                        cc = ((b % 2) * 2 + half) * P
                        mm = e.transpose(bank[2 + n % 2][:, cc:cc + P], lg[i % 2][:, b, half * P:half * P + P], ident[:, :])
                mm.then_inc(at_["t_done"], 1)

            def values(i, q):
                g, hp, j = (i % 6) // 2, i % 2, i // 6
                n, h = 4 * i + q, 2 * j + hp
                e.wait_ge(at_["pt"], n + 1)
                if hp == 0 and q == 0 and i > 0:
                    e.wait_ge(at_["o_free"], i // 2)
                for b in (2 * q, 2 * q + 1):
                    halves = (0, 1) if PREV[g][b] else (1,)
                    for half in halves:
                        cc = ((b % 2) * 2 + half) * P
                        mm = e.matmul(bank[4 + b // 4][64 * hp:64 * hp + 64, (b % 4) * P:(b % 4 + 1) * P],
                                      v_sb[g][:, b - 1 + half, 64 * h:64 * h + 64], pt[n % 2][:, cc:cc + P],
                                      start=(half == halves[0]), stop=(half == 1))
                mm.then_inc(at_["pv"], 1)

            def sample_values(n):
                s, k = n % 4, n // 4
                e.wait_ge(landed[s], 16 * (n_land("att", s, k) + 1))
                m = n - 18
                for pr in range(2):
                    if m < 16:
                        g, q0 = 1 + m // 8, TS_ * (m % 8)
                        for t in range(TS_):
                            cc = ((2 * g + pr) * TSAM + q0 + t) * 2
                            mm = e.matmul(bank[7][:, cc:cc + 2], w_raw[s][:, t * 256 + pr * P:t * 256 + pr * P + P],
                                          pc[:, cc:cc + 2], start=False, stop=(m == 17), skip_group_check=True)
                    else:
                        for nn in range(4):
                            cc = (pr * TSAM + TS_ * (4 * (m - 16) + nn)) * 2
                            mm = e.matmul(bank[7][:, cc:cc + 8], w_raw[s][:, nn * 256 + pr * P:nn * 256 + pr * P + P],
                                          pc[:, cc:cc + 8], start=False, stop=(m == 17), skip_group_check=True)
                mm.then_inc(att_used[s], 1)

            nv = 18
            scores(0)
            for i in range(12):
                g, j = (i % 6) // 2, i // 6
                if i < 11:
                    scores(i + 1)
                if i % 2 == 0 and j == 0:
                    for a in ((1,), (4,), (5, 6))[g]:
                        e.wait_ge(att_in[a], 16)
                turn(i, 0)
                for q in range(4):
                    if q < 3:
                        turn(i, q + 1)
                    values(i, q)
                for _ in range(2 if i < 6 else 1):
                    sample_values(nv)
                    nv += 1
                if i == 11:
                    e.wait_ge(att_used[3], 9)
                    e.nop().then_inc(at_["osam"], 1)
                if i % 6 == 5:
                    e.wait_ge(at_["lse"], j + 1)
                    for n in range(6 * j, 6 * j + 6):
                        gg, hb = (n % 6) // 2, n % 2
                        if n:
                            e.wait_ge(at_["ls"], n)
                        for b in range(4):
                            bb = 4 * hb + b
                            for hp in range(2):
                                mm = e.matmul(bank[6][64 * hp:64 * hp + 64, b * P:b * P + P],
                                              stat[:, 2, 6 * j + 2 * gg + hp, bb:bb + 1].to_broadcast([P, 64]),
                                              ident[:, :], start=True, stop=True)
                        mm.then_inc(at_["lb"], 1)

        @block.tensor
        def _(e):
            e.wait_ge(params[2], 16)
            e.wait_ge(consts, 1)
            e.wait_ge(c_sem, 1)
            mod_group(e, 0)
            mod_turn(e, 0, 0)
            pe_sum(e, 0, tb[1], (sq_added, 8))
            pe_wide(e, 4, (col_inv, 1))
            for g in range(1, 4):
                mod_group(e, g)
                mod_turn(e, g, g % 2)

            def w1_pe(i):
                for mm in range(2):
                    m = 2 * i + mm
                    first = isinstance(m, int) and m == 0
                    if first:
                        product_pair(e, "w1", 0, 0, first=True)
                    for s in (A0, A1):
                        if not first:
                            product(e, "w1", s, m, s, m, h_hi, h_lo)
                        if not (isinstance(m, int) and m + s == 0):
                            mod_turn(e, 2 * m + 3 + s, (3 + s) % 2)
                        mod_group(e, 2 * m + 4 + s)

            w1_pe(0)
            with e.Fori(1, 4) as i:
                w1_pe(i)
            mod_turn(e, 19, 1)
            for g in range(20, 25):
                mod_group(e, g)
                mod_turn(e, g, g % 2)
            pe_sum(e, 1, ysum, (conv_done, 8))
            pe_wide(e, 0, (mean_col, 1))
            for g in range(25, 28):
                mod_group(e, g)
                mod_turn(e, g, g % 2)
            pe_sum(e, 2, ysq, (sq_added, 16))
            pe_wide(e, 4, (col_inv, 2))
            product_pair(e, "w2", JB["w2"], 1)
            for m in range(2, KD):
                product(e, "w2", m % 4, m // 4, m % 2, JB["w2"] + m // 2, h_hi, h_lo)
            pe_sum(e, 3, acc, (sq_added, 24))
            pe_wide(e, 4, (col_inv, 3))
            pe_ffn(e, 0, 2)
            pe_sum(e, 4, acc, (sq_added, 32))
            pe_wide(e, 4, (col_inv, 4))
            def turn_values(c):
                e.wait_ge(job_free[c % 2], JB["k"] + (c + 6) // 2 + 1)
                for part in range(3):
                    n = 3 * c + part
                    if n >= 2:
                        e.wait_ge(v_free[n % 2], n // 2)
                    if part == 2:
                        mm = e.transpose(bank[6 + n % 2][0:TSAM, 0:P], kst[c % 2][:, TP:T], ident[:, :])
                    else:
                        for b in range(4):
                            t0 = (4 * part + b) * P
                            mm = e.transpose(bank[6 + n % 2][:, b * P:(b + 1) * P], kst[c % 2][:, t0:t0 + P], ident[:, :])
                    mm.then_inc(v_done, 1)

            product_pair(e, "kv", JB["k"], 3)
            for c in range(2, 12):
                product(e, "kv", c % 4, c // 4, c % 2, JB["k"] + c // 2, h_hi, h_lo)
                if c > 6:
                    turn_values(c - 7)
            turn_values(5)
            product_pair(e, "q", JB["q"], 4)
            for c in range(2, 6):
                product(e, "q", c % 4, c // 4, c % 2, JB["q"] + c // 2, h_hi, h_lo)
            pe_attention(e)
            for s in (A0, A1):
                e.wait_ge(split[s], n_split("wo", s, 0) + 1)
                e.wait_ge(job_free[s], JB["wo"])
            for pair in range(2):
                e.wait_ge(at_["o_ready"], 5 if pair == 0 else 8)
                for s in (A0, A1):
                    for kk in (pair, 2 + pair, 4 + pair):
                        for q, (w, a) in enumerate(((w_hi, o_hi), (w_hi, o_lo), (w_lo, o_hi))):
                            for c in range(NC):
                                mm = e.matmul(bank[3 * s + c][:, 0:CW], w[s][:, kk * P:(kk + 1) * P],
                                              a[:, kk, c * CW:(c + 1) * CW], start=(kk == 0 and q == 0),
                                              stop=(kk == 5 and q == 2))
                    if pair == 1:
                        mm.then_inc(used[s], 1)
            for m in range(2, KD):
                product(e, "wo", m % 4, m // 4, m % 2, JB["wo"] + m // 2, o_hi, o_lo, nk=6)
            pe_sum(e, 5, acc, (sq_added, 40))
            pe_wide(e, 4, (col_inv, 5))
            pe_ffn(e, 1, 5)
            pe_sum(e, 6, acc, (sq_added, 48))
            pe_wide(e, 4, (col_inv, 6))


def m_unit(w, m):
    k = w.shape[0] // P
    return w[:, m * P:(m + 1) * P].reshape(k, P, P).transpose(1, 0, 2).reshape(P, k * P)


def stream(i):
    units = []
    for m in range(8):
        units += [m_unit(i["a_w1"][0], 8 + m), m_unit(i["a_w1"][0], m)]
    units += [m_unit(i["a_w2"][0], m) for m in range(8)]

    def ffn(l):
        up = [[m_unit(i["f_wup"][l], j), m_unit(i["f_wup"][l], NJ + j)] for j in range(NJ)]
        dn = [i["f_wdown"][l][j * P:(j + 1) * P] for j in range(NJ)]
        out = up[0] + up[1]
        for f in range(1, NG):
            out += up[2 * f] + dn[2 * f - 2:2 * f] + up[2 * f + 1]
        return out + dn[NJ - 2:]

    units += ffn(0)
    units += [m_unit(i["w_kv"], c) for c in range(12)]
    units += [m_unit(i["w_q"][0], c) for c in range(6)]
    for m in range(8):
        units.append(np.concatenate([m_unit(i["w_o"][0], m), np.zeros((P, 256), np.float32)], axis=1))
    units += ffn(1)
    return np.stack(units)


def mod_units(i):
    w = np.concatenate([i["w_mod"][0], i["w_mod_kv"], i["w_mod"][1]], axis=1)
    return w.reshape(4, 2, P, NMOD // 4, 512).transpose(3, 0, 2, 1, 4).reshape(NMOD, P, UNIT)


def chunks(v):
    return v.reshape(-1, P).T


def buckets(dist):
    d = np.maximum(dist, 1).astype(np.float32)
    large = 16 + (np.log(d / np.float32(16)) / np.float32(np.log(128.0)) * np.float32(16)).astype(np.int32)
    return np.where(dist < 16, dist, np.minimum(large, 31))


def bias_places():
    q, k = np.arange(P)[:, None], np.arange(2 * P)[None, :]
    at_p = []
    for g, dil in enumerate(DIL):
        m = q + P - k
        ok = (m >= 0) & (m <= SPAN)
        if g == 2:
            ok = ok & (k >= P) & (q // 64 == (k - P) // 64)
        at_p.append(np.where(ok, buckets(np.where(ok, m, 0) * dil), 32))
    tok, key = np.arange(TSAM)[:, None], np.arange(P + TSAM)[None, :]
    n, t = tok // TS_, tok % TS_
    at_s = []
    for g, dil in enumerate(DIL):
        new = key >= P
        kn, kt = (key - P) // TS_, (key - P) % TS_
        if g == 0:
            m = np.where(new, t - kt, P + t - key)
            ok = (m >= 0) & (m <= SPAN) & (~new | (kn == n))
        else:
            m = np.where(new, 0, P - key)
            ok = ~new | ((kn == n) & (kt == t))
        at_s.append(np.where(ok, buckets(np.where(ok, m, 0) * dil), 32))
    return np.stack(at_p), at_s


def cache_units(caches):
    units = []
    for kv in range(2):
        for g in (1, 2):
            d = DIL[g]
            c = caches[g][:, :, kv].reshape(NS, P, d, 256)[:, :, 0:TS_]
            for n in range(NS):
                if kv == 0:
                    units.append(c[n].reshape(P, TS_, 2, P).transpose(3, 2, 1, 0).reshape(P, UNIT))
                else:
                    units.append(c[n].reshape(P, UNIT))
        c = caches[0][:, :, kv].reshape(NS, P, 256)
        for n4 in range(2):
            cc = c[4 * n4:4 * n4 + 4]
            if kv == 0:
                units.append(cc.reshape(4, P, 2, P).transpose(3, 0, 2, 1).reshape(P, UNIT))
            else:
                units.append(cc.transpose(1, 0, 2).reshape(P, UNIT))
    return np.stack(units)


def lay_out(i):
    i = {k: np.asarray(v) for k, v in i.items()}
    xa = np.concatenate([i["x_prompt"][0], i["x_sample"].reshape(TSAM, D)], axis=0)
    c = np.concatenate([i["c_prompt"], i["c_sample"], np.zeros((1, D), np.float32)], axis=0)
    prm = [chunks(i["b_mod"][0]), chunks(i["b_mod_kv"]), chunks(i["b_mod"][1]), chunks(i["norm_mix"][0]),
           chunks(i["norm_ffn"][0]), chunks(i["norm_kv"]), chunks(i["norm_mix"][1]), chunks(i["norm_ffn"][1]),
           chunks(i["norm_f"]), chunks(i["a_b1"][0]), chunks(i["a_dwb"][0]), chunks(i["a_ln_g"][0]),
           chunks(i["a_ln_b"][0]), chunks(i["a_b2"][0]),
           i["a_dw"][0].reshape(CA, KD, P).transpose(2, 1, 0).reshape(P, KD * CA)]
    cwb = np.stack([np.stack([*i["f_cw"][l].reshape(3, 2 * NJ, P), i["f_cb"][l].reshape(2 * NJ, P)]) for l in range(2)])
    rel = np.concatenate([i["rel_bias"], np.full((1, 12), NEG, np.float32)], axis=0)
    at_p, at_s = bias_places()
    bias_p = rel[at_p].transpose(3, 0, 1, 2)
    bias_p = np.stack([np.stack([bias_p[4 * g + 2 * j + hp, g] for hp in range(2)], axis=1)
                       for j in range(2) for g in range(3)])
    bias_s = np.stack([np.concatenate([
        np.stack([rel[at_s[g], 4 * g + 2 * j + hp] for hp in range(2)], axis=1).reshape(64, 160)
        for j in range(2)]) for g in range(3)], axis=1)
    caches = [i["cache_kv_w128"], i["cache_kv_w512"], i["cache_kv_w2048"]]
    d = {
        "bias_p": bias_p, "bias_s": bias_s, "att": cache_units(caches),
        "cache0": caches[0].reshape(NS, -1), "cache1": caches[1].reshape(NS, -1), "cache2": caches[2].reshape(NS, -1),
        "ws": stream(i), "wm": mod_units(i),
        "xt": xa.reshape(T, KD, P).transpose(2, 1, 0),
        "ct": c.reshape(10, KD, P).transpose(2, 1, 0),
        "prm": np.concatenate(prm, axis=1),
        "cwb": cwb.transpose(0, 3, 2, 1),
        "hist_a": i["state_conv_a"][0].reshape(NS, HA, KD, P).transpose(2, 3, 0, 1).reshape(KD, P, NS * HA),
        "hist_f": i["state_conv_ffn"].reshape(2, NS, 2, 2 * NJ, P).transpose(0, 4, 3, 1, 2).reshape(2, P, 2 * NJ, 16),
        "ident": np.eye(P, dtype=np.float32),
    }
    return {k: np.ascontiguousarray(v) for k, v in d.items()}


OUTS = {"yt": (P, KD, T), "cap": (KD, P, 9 * HA), "cfo": (2, P, 2 * NJ, 18), "kt": (6, P, T), "v": (T, 768),
        "kvs0": (NS, (SPAN - TS_) * 512), "kvs1": (NS, (4 * SPAN - TS_) * 512), "kvs2": (NS, (16 * SPAN - TS_) * 512),
        "kvz": (4, P, UNIT)}


def assemble(o):
    y = o["yt"].transpose(2, 1, 0).reshape(T, D)
    keys = [o["kt"][2 * g:2 * g + 2].reshape(2, 2, 64, T) for g in range(3)]
    vals = [o["v"][:, 256 * g:256 * g + 256].reshape(T, 4, 64) for g in range(3)]
    prompt, sample = [], []
    for g, d in enumerate(DIL):
        k = keys[g]
        kp = k[..., :TP].reshape(2, 2, 64, d, TP // d).transpose(4, 3, 0, 1, 2).reshape(TP, 4, 64)
        kv = np.stack([kp, vals[g][:TP]], axis=1)
        w = SPAN * d
        if w <= TP:
            prompt.append(kv[TP - w:][None])
        else:
            pad = o["kvz"].reshape(w - TP, 2, 4, 64)
            prompt.append(np.concatenate([pad, kv], axis=0)[None])
        ks = k[..., TP:].transpose(3, 0, 1, 2).reshape(NS, TS_, 4, 64)
        new = np.stack([ks, vals[g][TP:].reshape(NS, TS_, 4, 64)], axis=2)
        sample.append(np.concatenate([o[f"kvs{g}"].reshape(NS, w - TS_, 2, 4, 64), new], axis=1))
    cap, cfo = o["cap"], o["cfo"]
    conv_a_p = cap[:, :, :HA].transpose(2, 0, 1).reshape(1, 1, HA, D)
    conv_a_s = cap[:, :, HA:].reshape(KD, P, NS, HA).transpose(2, 3, 0, 1).reshape(1, NS, HA, D)
    conv_f_p = cfo[..., :2].transpose(0, 3, 2, 1).reshape(2, 1, 2, 2 * DFF)
    conv_f_s = cfo[..., 2:].reshape(2, P, 2 * NJ, NS, 2).transpose(0, 3, 4, 2, 1).reshape(2, NS, 2, 2 * DFF)
    return (y[:TP][None], y[TP:].reshape(NS, TS_, D), *prompt, conv_a_p, conv_f_p, *sample, conv_a_s, conv_f_s)


def kernel(**inputs):
    import concourse.bacc as _bacc
    from concourse.bass_utils import run_bass_kernel_spmd as _run

    d = lay_out(inputs)
    nc = _bacc.Bacc("TRN2", target_bir_lowering=False, num_devices=1)
    ins = {k: nc.dram_tensor(f"in_{k}", a.shape, F, kind="ExternalInput").ap() for k, a in d.items()}
    outs = {k: nc.dram_tensor(f"out_{k}", s, F, kind="ExternalOutput").ap() for k, s in OUTS.items()}
    program(nc, ins, outs)
    r = _run(nc, [{f"in_{k}": a for k, a in d.items()}], core_ids=[0])
    return assemble({k: r.results[0][f"out_{k}"] for k in OUTS})
```
